# Optimizing a Trainium2 kernel written in Bass

```python
import functools
import jax, jax.numpy as jnp
from jax import lax
import numpy as np

D_MODEL = 1024
BATCH = 1
SEQ = 512
DEPTH = 2
DEC_BATCH = 8
DEC_SEQ = 4
PAST_LEN = 2048
PAGE_SIZE = 128

HEAD_DIM = 64
N_HEADS_A = 6
D_A = N_HEADS_A * HEAD_DIM
D_B = 384
N_BLOCKS_B = 6
BLOCK_B = D_B // N_BLOCKS_B
N_HEADS_C = 4
DK_C = 64
DV_C = 64
D_C = N_HEADS_C * DV_C
D_MIX = D_A + D_B + D_C
DILATED_CONFIGS = ((128, 1), (512, 4), (2048, 16))
MAX_WINDOW = 2048
LOCAL_BLK = 128
CONV_W = 4
LRU_C = 8.0
MLSTM_CHUNK = 128
D_FF = 2816
D_PLE = 256
EPS = 1e-6
NEG = -1e30
SPLIT_SIZES = (D_A, D_A, D_A, D_B, D_B, D_C, D_C, D_C, D_C, N_HEADS_C, N_HEADS_C)
SPLIT_IDX = tuple(int(s) for s in np.cumsum(SPLIT_SIZES)[:-1])
N_IN = int(sum(SPLIT_SIZES))

kernel_name = "hybrid_dilated_rglru_mlstm_step"

def _rms(x, g):
    xf = x.astype(jnp.float32)
    y = xf * lax.rsqrt(jnp.mean(jnp.square(xf), axis=-1, keepdims=True) + EPS)
    return (y * g.astype(jnp.float32)).astype(x.dtype)

def _swiglu(x, wg, wu, wd):
    return (jax.nn.silu(x @ wg) * (x @ wu)) @ wd

def _dilated_prompt(q, k, v, window, dil):
    B, S, H, Dh = q.shape
    L = S // dil
    nb = -(-L // LOCAL_BLK)
    Lp = nb * LOCAL_BLK
    n_back = window // dil

    def to_blocks(t):
        t = t.reshape(B, L, dil, H, Dh)
        t = jnp.pad(t, ((0, 0), (0, Lp - L), (0, 0), (0, 0), (0, 0)))
        return t.reshape(B, nb, LOCAL_BLK, dil, H, Dh)

    def with_prev(t):
        prev = jnp.pad(t, ((0, 0), (1, 0), (0, 0), (0, 0), (0, 0), (0, 0)))[:, :nb]
        return jnp.concatenate([prev, t], axis=2)

    qb = to_blocks(q)
    kb = with_prev(to_blocks(k))
    vb = with_prev(to_blocks(v))
    s = jnp.einsum('bnqrhd,bnkrhd->bnrhqk', qb, kb).astype(jnp.float32) * (Dh ** -0.5)
    qi = jnp.arange(LOCAL_BLK)[:, None]
    ki = jnp.arange(2 * LOCAL_BLK)[None, :]
    dist = LOCAL_BLK + qi - ki
    band = (dist >= 0) & (dist <= n_back)
    not_first = jnp.arange(nb)[:, None, None] > 0
    valid = band[None] & (not_first | (ki >= LOCAL_BLK)[None])
    valid = valid[None, :, None, None]
    s = jnp.where(valid, s, NEG)
    m = jnp.max(s, axis=-1)
    p = jnp.where(valid, jnp.exp(s - m[..., None]), 0.0)
    den = jnp.sum(p, axis=-1)
    num = jnp.einsum('bnrhqk,bnkrhd->bnqrhd', p, vb.astype(jnp.float32))
    num = num.reshape(B, Lp, dil, H, Dh)[:, :L].reshape(B, S, H, Dh)

    def stat(t):
        return jnp.transpose(t, (0, 1, 4, 2, 3)).reshape(B, Lp, dil, H)[:, :L].reshape(B, S, H)

    return num, stat(m), stat(den)

def _dilated_sample(q, kc, vc, window, dil):
    B, T, H, Dh = q.shape
    W = kc.shape[1] - T
    n = window // dil + 1
    idx = W + jnp.arange(T)[:, None] - dil * jnp.arange(n)[None, :]
    valid = (idx >= 0)[None, :, None, :]
    flat = jnp.maximum(idx, 0).reshape(-1)
    kg = jnp.take(kc, flat, axis=1).reshape(B, T, n, H, Dh)
    vg = jnp.take(vc, flat, axis=1).reshape(B, T, n, H, Dh)
    s = jnp.einsum('bthd,btnhd->bthn', q, kg).astype(jnp.float32) * (Dh ** -0.5)
    s = jnp.where(valid, s, NEG)
    m = jnp.max(s, axis=-1)
    p = jnp.where(valid, jnp.exp(s - m[..., None]), 0.0)
    den = jnp.sum(p, axis=-1)
    num = jnp.einsum('bthn,btnhd->bthd', p, vg.astype(jnp.float32))
    return num, m, den

def _combine(parts):
    M = functools.reduce(jnp.maximum, [m for _, m, _ in parts])
    num = sum(nm * jnp.exp(m - M)[..., None] for nm, m, _ in parts)
    den = sum(d * jnp.exp(m - M) for _, m, d in parts)
    return num / den[..., None]

def _lin_op(left, right):
    a1, b1 = left
    a2, b2 = right
    return a1 * a2, a2 * b1 + b2

def _rglru(xb, conv_buf, h0, w):
    B, T, _ = xb.shape
    xp = jnp.concatenate([conv_buf.astype(xb.dtype), xb], axis=1)
    xc = w['conv_b'] + sum(xp[:, j:j + T] * w['conv_w'][j] for j in range(CONV_W))
    new_buf = xp[:, T:]
    xr = xc.reshape(B, T, N_BLOCKS_B, BLOCK_B)
    r = jax.nn.sigmoid(jnp.einsum('btnc,ncd->btnd', xr, w['w_rg_a']).reshape(B, T, D_B) + w['b_rg_a'])
    i = jax.nn.sigmoid(jnp.einsum('btnc,ncd->btnd', xr, w['w_rg_x']).reshape(B, T, D_B) + w['b_rg_x'])
    log_a = -LRU_C * r.astype(jnp.float32) * jax.nn.softplus(-w['lru_lambda'].astype(jnp.float32))
    a = jnp.exp(log_a)
    b = jnp.sqrt(-jnp.expm1(2.0 * log_a)) * (i * xc).astype(jnp.float32)
    b = b.at[:, 0].add(a[:, 0] * h0.astype(jnp.float32))
    _, h = lax.associative_scan(_lin_op, (a, b), axis=1)
    return h, h[:, -1], new_buf

def _mlstm_chunk(carry, inp):
    C, n, m = carry
    q, k, v, ig, lf = inp
    L = q.shape[1]
    b = jnp.cumsum(lf, axis=1)
    Dm = b[:, :, None, :] - b[:, None, :, :] + ig[:, None, :, :]
    causal = jnp.tril(jnp.ones((L, L), dtype=bool))[None, :, :, None]
    Dm = jnp.where(causal, Dm, NEG)
    inter = b + m[:, None, :]
    mt = jnp.maximum(inter, jnp.max(Dm, axis=2))
    Wt = jnp.exp(Dm - mt[:, :, None, :])
    wi = jnp.exp(inter - mt)
    A = Wt * jnp.einsum('bthd,bshd->btsh', q, k)
    num = jnp.einsum('btsh,bshd->bthd', A, v) + wi[..., None] * jnp.einsum('bthk,bhkv->bthv', q, C)
    den = jnp.sum(A, axis=2) + wi * jnp.einsum('bthk,bhk->bth', q, n)
    h = num / jnp.maximum(jnp.abs(den), jnp.exp(-mt))[..., None]
    m_new = mt[:, -1]
    ws = jnp.exp(b[:, -1:] - b + ig - m_new[:, None])
    wc = jnp.exp(b[:, -1] + m - m_new)
    C_new = wc[..., None, None] * C + jnp.einsum('bsh,bshk,bshv->bhkv', ws, k, v)
    n_new = wc[..., None] * n + jnp.einsum('bsh,bshk->bhk', ws, k)
    return (C_new, n_new, m_new), h

def _mlstm(q, k, v, ig, lf, C0, n0, m0):
    B, T = q.shape[:2]
    chunk = MLSTM_CHUNK if T % MLSTM_CHUNK == 0 else T
    nc = T // chunk

    def split(t):
        t = t.astype(jnp.float32)
        return jnp.moveaxis(t.reshape((B, nc, chunk) + t.shape[2:]), 1, 0)

    xs = (split(q), split(k), split(v), split(ig), split(lf))
    (C, n, m), h = lax.scan(_mlstm_chunk, (C0, n0, m0), xs)
    h = jnp.moveaxis(h, 0, 1).reshape(B, T, N_HEADS_C, DV_C)
    return h, C, n, m

def _token_mixing(u, w, cache):
    B, T, _ = u.shape
    z = u @ w['w_in']
    qa, ka, va, xb, gb, qc, kc, vc, oc, ic, fc = jnp.split(z, SPLIT_IDX, axis=-1)
    qa = qa.reshape(B, T, N_HEADS_A, HEAD_DIM)
    ka = ka.reshape(B, T, N_HEADS_A, HEAD_DIM)
    va = va.reshape(B, T, N_HEADS_A, HEAD_DIM)
    if cache is None:
        parts = [_dilated_prompt(qa, ka, va, wd, dl) for wd, dl in DILATED_CONFIGS]
        keep = min(MAX_WINDOW, T)
        new_k, new_v = ka[:, T - keep:], va[:, T - keep:]
        conv_buf = jnp.zeros((B, CONV_W - 1, D_B), u.dtype)
        h0 = jnp.zeros((B, D_B), jnp.float32)
        C0 = jnp.zeros((B, N_HEADS_C, DK_C, DV_C), jnp.float32)
        n0 = jnp.zeros((B, N_HEADS_C, DK_C), jnp.float32)
        m0 = jnp.zeros((B, N_HEADS_C), jnp.float32)
    else:
        k_cache, v_cache, conv_buf, h0, C0, n0, m0 = cache
        kcat = jnp.concatenate([k_cache.astype(ka.dtype), ka], axis=1)
        vcat = jnp.concatenate([v_cache.astype(va.dtype), va], axis=1)
        parts = [_dilated_sample(qa, kcat, vcat, wd, dl) for wd, dl in DILATED_CONFIGS]
        new_k, new_v = ka, va
    ya = _rms(_combine(parts).reshape(B, T, D_A).astype(u.dtype), w['g_out_a'])
    hb, hT, new_buf = _rglru(xb, conv_buf, h0, w)
    yb = _rms(jax.nn.gelu(gb) * hb.astype(u.dtype), w['g_out_b'])
    qc = qc.reshape(B, T, N_HEADS_C, DK_C)
    kc = kc.reshape(B, T, N_HEADS_C, DK_C) * (DK_C ** -0.5)
    vc = vc.reshape(B, T, N_HEADS_C, DV_C)
    igc = ic.astype(jnp.float32) + w['b_mlstm_i'].astype(jnp.float32)
    lfc = jax.nn.log_sigmoid(fc.astype(jnp.float32) + w['b_mlstm_f'].astype(jnp.float32))
    hc, C1, n1, m1 = _mlstm(qc, kc, vc, igc, lfc, C0.astype(jnp.float32),
                            n0.astype(jnp.float32), m0.astype(jnp.float32))
    hc = jax.nn.sigmoid(oc).reshape(B, T, N_HEADS_C, DV_C) * hc.astype(u.dtype)
    yc = _rms(hc, w['g_out_c'].reshape(N_HEADS_C, DV_C)).reshape(B, T, D_C)
    y = jnp.concatenate([ya, yb, yc], axis=-1) @ w['w_out']
    return y, (new_k, new_v, new_buf, hT, C1, n1, m1)

def _layer(x, pe, w, cache):
    f1 = _swiglu(_rms(x, w['g_f1_pre']), w['w_f1_gate'], w['w_f1_up'], w['w_f1_down'])
    x = x + 0.5 * _rms(f1, w['g_f1_post'])
    ymix, st = _token_mixing(_rms(x, w['g_mix_pre']), w, cache)
    x = x + _rms(ymix, w['g_mix_post'])
    f2 = _swiglu(_rms(x, w['g_f2_pre']), w['w_f2_gate'], w['w_f2_up'], w['w_f2_down'])
    x = x + 0.5 * _rms(f2, w['g_f2_post'])
    gate = jax.nn.sigmoid(_rms(x, w['g_ple_pre']) @ w['w_ple_gate'])
    x = x + _rms(gate * (pe.astype(x.dtype) @ w['w_ple_proj']), w['g_ple_post'])
    return x, st

def setup_inputs(seed: int = 0) -> dict:
    key = jax.random.key(seed)
    keys = iter(jax.random.split(key, 64))
    f32 = jnp.float32

    def nrm(shape, scale):
        return jax.random.normal(next(keys), shape, f32) * scale

    def gain(shape):
        return 1.0 + nrm(shape, 0.02)

    W_BUF = min(MAX_WINDOW, PAST_LEN)
    u = jax.random.uniform(next(keys), (DEPTH, D_B), f32, minval=0.9, maxval=0.999)
    s = u ** (1.0 / LRU_C)
    lam = jnp.log(s) - jnp.log1p(-s)
    return {
        'x_prompt': nrm((BATCH, SEQ, D_MODEL), 1.0),
        'x_sample': nrm((DEC_BATCH, DEC_SEQ, D_MODEL), 1.0),
        'cache_k': nrm((DEPTH, DEC_BATCH, W_BUF, N_HEADS_A, HEAD_DIM), 1.0),
        'cache_v': nrm((DEPTH, DEC_BATCH, W_BUF, N_HEADS_A, HEAD_DIM), 1.0),
        'state_conv': nrm((DEPTH, DEC_BATCH, CONV_W - 1, D_B), 1.0),
        'state_h': nrm((DEPTH, DEC_BATCH, D_B), 0.5),
        'state_C': nrm((DEPTH, DEC_BATCH, N_HEADS_C, DK_C, DV_C), 0.3),
        'state_n': nrm((DEPTH, DEC_BATCH, N_HEADS_C, DK_C), 0.3),
        'state_m': nrm((DEPTH, DEC_BATCH, N_HEADS_C), 1.0),
        'p_prompt': nrm((DEPTH, BATCH, SEQ, D_PLE), 1.0),
        'p_sample': nrm((DEPTH, DEC_BATCH, DEC_SEQ, D_PLE), 1.0),
        'g_f1_pre': gain((DEPTH, D_MODEL)),
        'w_f1_gate': nrm((DEPTH, D_MODEL, D_FF), D_MODEL ** -0.5),
        'w_f1_up': nrm((DEPTH, D_MODEL, D_FF), D_MODEL ** -0.5),
        'w_f1_down': nrm((DEPTH, D_FF, D_MODEL), D_FF ** -0.5),
        'g_f1_post': gain((DEPTH, D_MODEL)),
        'g_mix_pre': gain((DEPTH, D_MODEL)),
        'w_in': nrm((DEPTH, D_MODEL, N_IN), D_MODEL ** -0.5),
        'conv_w': nrm((DEPTH, CONV_W, D_B), CONV_W ** -0.5),
        'conv_b': nrm((DEPTH, D_B), 0.01),
        'w_rg_a': nrm((DEPTH, N_BLOCKS_B, BLOCK_B, BLOCK_B), BLOCK_B ** -0.5),
        'b_rg_a': nrm((DEPTH, D_B), 0.01),
        'w_rg_x': nrm((DEPTH, N_BLOCKS_B, BLOCK_B, BLOCK_B), BLOCK_B ** -0.5),
        'b_rg_x': nrm((DEPTH, D_B), 0.01),
        'lru_lambda': lam,
        'b_mlstm_i': nrm((DEPTH, N_HEADS_C), 0.1),
        'b_mlstm_f': jnp.linspace(3.0, 6.0, N_HEADS_C, dtype=f32)[None] + nrm((DEPTH, N_HEADS_C), 0.1),
        'g_out_a': gain((DEPTH, D_A)),
        'g_out_b': gain((DEPTH, D_B)),
        'g_out_c': gain((DEPTH, D_C)),
        'w_out': nrm((DEPTH, D_MIX, D_MODEL), D_MIX ** -0.5),
        'g_mix_post': gain((DEPTH, D_MODEL)),
        'g_f2_pre': gain((DEPTH, D_MODEL)),
        'w_f2_gate': nrm((DEPTH, D_MODEL, D_FF), D_MODEL ** -0.5),
        'w_f2_up': nrm((DEPTH, D_MODEL, D_FF), D_MODEL ** -0.5),
        'w_f2_down': nrm((DEPTH, D_FF, D_MODEL), D_FF ** -0.5),
        'g_f2_post': gain((DEPTH, D_MODEL)),
        'g_ple_pre': gain((DEPTH, D_MODEL)),
        'w_ple_gate': nrm((DEPTH, D_MODEL, D_MODEL), D_MODEL ** -0.5),
        'w_ple_proj': nrm((DEPTH, D_PLE, D_MODEL), D_PLE ** -0.5),
        'g_ple_post': gain((DEPTH, D_MODEL)),
    }

def reference(x_prompt, x_sample, cache_k, cache_v, state_conv, state_h, state_C, state_n, state_m,
              p_prompt, p_sample, g_f1_pre, w_f1_gate, w_f1_up, w_f1_down, g_f1_post, g_mix_pre,
              w_in, conv_w, conv_b, w_rg_a, b_rg_a, w_rg_x, b_rg_x, lru_lambda, b_mlstm_i, b_mlstm_f,
              g_out_a, g_out_b, g_out_c, w_out, g_mix_post, g_f2_pre, w_f2_gate, w_f2_up, w_f2_down,
              g_f2_post, g_ple_pre, w_ple_gate, w_ple_proj, g_ple_post):
    xp, xs = x_prompt, x_sample
    sp = [[] for _ in range(7)]
    ss = [[] for _ in range(7)]
    for i in range(DEPTH):
        w = dict(
            g_f1_pre=g_f1_pre[i], w_f1_gate=w_f1_gate[i], w_f1_up=w_f1_up[i], w_f1_down=w_f1_down[i],
            g_f1_post=g_f1_post[i], g_mix_pre=g_mix_pre[i], w_in=w_in[i], conv_w=conv_w[i],
            conv_b=conv_b[i], w_rg_a=w_rg_a[i], b_rg_a=b_rg_a[i], w_rg_x=w_rg_x[i], b_rg_x=b_rg_x[i],
            lru_lambda=lru_lambda[i], b_mlstm_i=b_mlstm_i[i], b_mlstm_f=b_mlstm_f[i],
            g_out_a=g_out_a[i], g_out_b=g_out_b[i], g_out_c=g_out_c[i], w_out=w_out[i],
            g_mix_post=g_mix_post[i], g_f2_pre=g_f2_pre[i], w_f2_gate=w_f2_gate[i],
            w_f2_up=w_f2_up[i], w_f2_down=w_f2_down[i], g_f2_post=g_f2_post[i],
            g_ple_pre=g_ple_pre[i], w_ple_gate=w_ple_gate[i], w_ple_proj=w_ple_proj[i],
            g_ple_post=g_ple_post[i])
        xp, st_p = _layer(xp, p_prompt[i], w, None)
        cache_i = (cache_k[i], cache_v[i], state_conv[i], state_h[i], state_C[i], state_n[i], state_m[i])
        xs, st_s = _layer(xs, p_sample[i], w, cache_i)
        for j in range(7):
            sp[j].append(st_p[j])
            ss[j].append(st_s[j])
    k_prompt, v_prompt, conv_prompt, h_prompt, C_prompt, n_prompt, m_prompt = [jnp.stack(a) for a in sp]
    k_sample, v_sample, conv_sample, h_sample, C_sample, n_sample, m_sample = [jnp.stack(a) for a in ss]
    return (xp, xs, k_prompt, v_prompt, k_sample, v_sample, conv_prompt, conv_sample,
            h_prompt, h_sample, C_prompt, C_sample, n_prompt, n_sample, m_prompt, m_sample)


_drawn_inputs = setup_inputs


def setup_inputs(seed=0):
    import zlib

    import numpy as np

    out = dict(_drawn_inputs(seed))
    spreads = {}
    factors = {'g_f1_post': 2.974,
     'b_rg_a': 24.224,
     'b_rg_x': 8.0,
     'g_out_a': 18.238,
     'g_out_b': 16.651,
     'g_out_c': 21.08,
     'g_mix_post': 3.218,
     'g_f2_pre': 5.156,
     'g_f2_post': 7.713,
     'g_ple_pre': 25.114,
     'g_ple_post': 11.722}
    for name, (base, spread) in spreads.items():
        noise = np.random.default_rng([zlib.crc32(name.encode()), seed]).standard_normal(out[name].shape)
        drawn = base * np.exp(spread * noise) if base else spread * noise
        out[name] = __import__('jax').numpy.asarray(drawn.astype(out[name].dtype))
    for name, factor in factors.items():
        out[name] = (out[name] * factor).astype(out[name].dtype)
    return out
```

```python
import numpy as np
from contextlib import ExitStack, contextmanager

import concourse.bass as bass
from concourse import mybir

F32 = mybir.dt.float32
F32R = mybir.dt.float32r
ALU = mybir.AluOpType
ACT = mybir.ActivationFunctionType
EXP_LN = "natural_log_exp_and_others"

P = 128
DEPTH, D, SEQ, NB, NT = 2, 1024, 512, 8, 4
TOK = SEQ + NB * NT
HALF = TOK // 2
DFF, HD, HA, HC, DB, DPLE = 2816, 64, 6, 4, 384, 256
KT = D // P
FT = DFF // P
W_BUF = 2048
KEYS = 512 + 384
KEYS_NEW = 16
KS = KEYS + KEYS_NEW
EPS = 1e-6
NEG = -1e30
LOW = -3.0e38
SCALE = HD ** -0.5

ZXB, ZGB, ZGATE, ZQC, ZKC, ZVC, ZOC, ZQ, ZK, ZV, NZ = 0, 3, 6, 7, 9, 11, 13, 15, 18, 21, 24
C_UP, C_DOWN, C_IN, C_OUT, C_PJ, C_PG = 2 * FT, 3 * KT, NZ, KT, 2, KT
CH_F1 = 0
CH_D1 = CH_F1 + C_UP
CH_IN = CH_D1 + C_DOWN
CH_OUT = CH_IN + C_IN
CH_F2 = CH_OUT + C_OUT
CH_D2 = CH_F2 + C_UP
CH_PJ = CH_D2 + C_DOWN
CH_PG = CH_PJ + C_PJ
CHUNKS = CH_PG + C_PG
DOWN_BLOCKS = (8, 7, 7)

(G_F1PRE, G_F1POST, G_MIXPRE, G_MIXPOST, G_F2PRE, G_F2POST, G_PLEPRE, G_PLEPOST) = range(0, 64, 8)
CONV_W, CONV_B, B_RA, B_RX, LAM, G_A, G_B, G_C, B_I, B_F, NPAR = 64, 76, 79, 82, 85, 88, 91, 94, 96, 97, 98
D_HALF1, D_HALF2, D_SPNEG, D_SPPOS, ND = 0, 8, 16, 19, 22
K_ID, K_ONE, K_BLK = 0, 128, 256
K_PADD, K_PMUL = 384, 896
K_SADD = 1408
K_SMUL = K_SADD + KS
K_SELH = K_SMUL + KS
K_SEL2 = K_SELH + 512
K_RST = K_SEL2 + 256
NCONST = K_RST + TOK
S_CP, S_CS, S_HP, S_HS, NSB = 0, 9, 81, 84, 108
GELU_1 = 2.0 * (2.0 / np.pi) ** 0.5
GELU_3 = GELU_1 * 0.044715

N_F1, N_MIX, N_OUT, N_F2, N_PLE = range(5)
OUT_TILES = (ZV, ZV + 1, ZV + 2, ZGB, ZGB + 1, ZGB + 2, ZVC, ZVC + 1)
LINKS_ACT, LINKS_DVE, LINKS_POOL, LINKS_PE = 13, 176, 1, 9


class Signal:

    def __init__(self, sem, per_layer, ahead=0, unit=1):
        self.sem, self.per, self.ahead, self.unit = sem, per_layer, ahead, unit

    def at(self, layer, n):
        return layer * (self.per * self.unit) + (n + self.ahead) * self.unit


class Steps:

    def __init__(self, eng, signal, layer):
        self.eng, self.s, self.layer = eng, signal, layer
        self.n = 0
        self.f, self.per_turn = 0, 0

    def link(self, ins, hold=False):
        ins.then_inc(self.s.sem, 1)
        self.n += 1
        self.eng.wait_ge(self.s.sem, self.s.at(self.layer, self.n + self.f * self.per_turn))
        if hold:
            self.eng.nop(nofuse=True)

    @contextmanager
    def loop(self, count, per_turn):
        with self.eng.Fori(0, count) as f:
            start = self.n
            self.f, self.per_turn = f, per_turn
            yield f
            assert self.n - start == per_turn, ("links in a turn", self.n - start)
            self.f, self.per_turn = 0, 0
            self.n = start + count * per_turn

    def end(self):
        assert self.n == self.s.per, (self.s.sem, "links in a layer", self.n, "stated", self.s.per)


def build(nc, I, O):
    x_in, weights, par, rgw, consts, pe_in = I["x"], I["weights"], I["par"], I["rgw"], I["consts"], I["pe"]
    ctx = ExitStack()
    with ctx:
        base = (nc.sbuf_base + 63) // 64 * 64
        here = [base]

        def place(name, shape, dt=F32, at=None):
            size = int(np.prod(shape[1:])) * 4
            offset = here[0] if at is None else at
            if at is None:
                here[0] += (size + 31) // 32 * 32
                assert here[0] <= nc.sbuf_usable_end, (name, here[0], nc.sbuf_usable_end)
            return nc.alloc_sbuf_tensor_at(name, shape, dt, offset=offset), offset, offset + (size + 31) // 32 * 32

        x, _, _ = place("x", [P, KT, 2, HALF])
        xh, a_xh, _ = place("xh", [P, KT, 2, HALF], F32R)
        xl, a_xl, e_xl = place("xl", [P, KT, 2, HALF], F32R)
        hh, a_h, _ = place("hh", [P, FT, 2, HALF], F32R)
        hl, _, e_h = place("hl", [P, FT, 2, HALF], F32R)
        raw, _, _ = place("raw", [P, 2, 8 * P])
        wh, _, _ = place("wh", [P, 2, 8 * P], F32R)
        wl, _, _ = place("wl", [P, 2, 8 * P], F32R)
        act_out, a_e, _ = place("act_out", [P, 2, 2, HALF])
        rstd, _, _ = place("rstd", [P, 2, HALF])
        acc, _, _ = place("acc", [P, 2, HALF])
        sq, a_sq, _ = place("sq", [P, 2, 2, HALF])
        tmp, a_tmp, _ = place("tmp", [P, 2, 2, HALF])
        con, _, _ = place("con", [P, NCONST])
        pc, _, _ = place("pc", [P, NPAR])
        dc, _, _ = place("dc", [P, ND])
        sp, _, _ = place("sp", [P, 5, 4])
        stat, _, _ = place("stat", [P, 2, 4])
        rg, _, _ = place("rg", [P, 2, 3, P])
        y_ff, _, _ = place("y_ff", [P, KT, 2, HALF], at=a_xl)
        z, _, a = place("z", [P, NZ, TOK], at=a_h)
        a_kv = a
        kv, _, e = place("kv", [P, 4, 7 * 384], at=a_kv)
        assert e <= e_h
        y_z, _, e = place("y_z", [P, KT, 2, HALF], at=a_h)
        pe_raw, _, e = place("pe_raw", [P, 2, 2, HALF], at=e)
        ph, _, e = place("ph", [P, 2, 2, HALF], F32R, at=e)
        pl, _, e = place("pl", [P, 2, 2, HALF], F32R, at=e)
        assert e <= e_h
        xc, _, e = place("xc", [P, 3, TOK], at=a_kv)
        gt, _, e = place("gt", [P, 3, 2, TOK], at=e)
        av, _, e = place("av", [P, 3, TOK], at=e)
        bv, _, e = place("bv", [P, 3, TOK], at=e)
        xs, _, e = place("xs", [P, 3, NB, 7], at=e)
        h0, _, e = place("h0", [P, 3, NB], at=e)
        sb_, _, e = place("sb", [P, NSB], at=e)
        ht, _, e = place("ht", [P, 3, NB], at=e)
        a_b2 = e
        rows, _, e = place("rows", [HC, 7, TOK], at=a_kv)
        LF, BR, GR, GG, MT, DW, FB = range(7)
        wi, _, e = place("wi", [P, 2, TOK], at=e)
        em, _, e = place("em", [P, 2, TOK], at=e)
        wt, _, e = place("wt", [P, HC, P], at=e)
        at_, _, e = place("at", [P, HC, P], at=e)
        gc, _, e = place("gc", [P, 5, HC], at=e)
        hc, _, e = place("hc", [P, 2, TOK], at=e)
        qw, _, e = place("qw", [P, 2, TOK], at=e)
        kw, _, e = place("kw", [P, HC, HD], at=e)
        dn, _, e = place("dn", [P, 2, P], at=e)
        mp, _, e = place("mp", [HC, 8], at=e)
        m0, _, e = place("m0", [HC, NB], at=e)
        mo, _, e = place("mo", [HC, 1 + NB], at=e)
        assert e <= e_h, (e, e_h)
        vt, _, e = place("vt", [P, 4, 384], at=a_xh)
        vs, _, e = place("vs", [KEYS_NEW, 2, 384], at=e)
        kc, _, e = place("kc", [P, 5, HC * HD], at=e)
        va, _, e = place("va", [P, 5, HC, HD + 1], at=e)
        cs, _, e = place("cs", [P, NB, 2, HD + 1], at=e)
        cp, _, e = place("cp", [P, 2, HD + 1], at=e)
        a_w = e
        kwm, _, e = place("kwm", [32, NB, HC, HD], at=a_w)
        assert e <= e_xl
        qbd, _, e = place("qbd", [P, NB, 3, 32], at=a_w)
        pts, _, e = place("pts", [P, 8, P], at=e)
        assert e <= e_xl, (e, e_xl)
        pp, _, _ = place("pp", [P, 2, SEQ], at=a_e)
        ptp, _, _ = place("ptp", [P, 2, 4, P], at=a_sq)
        ps_, _, _ = place("psm", [P, KS], at=a_tmp)
        ge, _, e = place("ge", [P, 3, TOK], at=a_sq)
        gr, _, _ = place("gr", [P, 4, 2, HALF], at=a_kv)

        psum = ctx.enter_context(nc.psum_tensor("psum", [P, 8, 512], F32))

        def T(i):
            return psum[:, 2 * i:2 * i + 2, 0:HALF]

        ident, ones, blk = con[:, K_ID:K_ID + P], con[:, K_ONE:K_ONE + P], con[:, K_BLK:K_BLK + P]

        def signal(name, per_layer, ahead=0, unit=1):
            return Signal(ctx.enter_context(nc.semaphore(name)), per_layer, ahead, unit)

        loaded = [signal(f"chunk_loaded_{s}", CHUNKS // 2, 0, 16) for s in range(2)]
        hi = signal("chunk_hi_ready", CHUNKS)
        lo = signal("chunk_lo_ready", CHUNKS)
        part_used = signal("down_part_used", 4 * KT)
        const_loaded = signal("const_loaded", 0, 0, 16)
        x_loaded = signal("x_loaded", 0, 0, 16)
        par_loaded = signal("par_loaded", 2, 0, 16)
        pe_loaded = signal("pe_loaded", 1, 0, 16)
        sb_loaded = signal("branch_state_loaded", 2, 0, 16)
        sc_loaded = signal("memory_state_loaded", 2, 0, 16)
        kv_loaded = [signal(f"kv_loaded_{s}", 4, 0, 16) for s in range(4)]
        z_stored = signal("kv_rows_stored", 2, 0, 16)
        sb_stored = signal("branch_state_stored", 1, 0, 16)
        sc_stored = signal("memory_state_stored", 3, 0, 16)
        x_stored = signal("x_stored", 0, 0, 16)
        layer_done = signal("layer_done", 1)
        sq_ready = signal("square_ready", 64, 8)
        sq_added = signal("square_added", 56, 7)
        stat_done = signal("mean_square_done", 8)
        rstd_ready = signal("rstd_ready", 8)
        n_ready = signal("normed_ready", 5 * KT)
        nh_ready = signal("normed_hi_ready", 5 * KT)
        nl_ready = signal("normed_lo_ready", 5 * KT)
        xn_ready = signal("x_ready", 32)
        gate_done = signal("gate_done", 2 * FT)
        up_done = signal("up_done", 2 * FT)
        silu_ready = signal("silu_ready", 2 * FT)
        h_ready = signal("h_ready", 2 * FT, 2)
        hh_ready = signal("h_hi_ready", 2 * FT)
        hl_ready = signal("h_lo_ready", 2 * FT, 2)
        out_done = signal("out_tile_done", 3 * KT)
        y_ready = signal("y_ready", 3 * KT, 4)
        z_done = signal("z_tile_done", NZ)
        z_ready = signal("z_ready", NZ, 2)
        p_ready = signal("pe_split_ready", 2)
        pj_done = signal("embedding_done", KT)
        pj_ready = signal("embedding_ready", KT)
        pg_done = signal("ple_gate_done", KT)
        pg_ready = signal("ple_gate_ready", KT, 2)
        ye_ready = signal("ple_y_ready", KT, 2)
        act_steps = signal("scalar_steps", LINKS_ACT)
        dve_steps = signal("vector_steps", LINKS_DVE)
        pe_steps = signal("tensor_steps", LINKS_PE)
        pool_steps = signal("pool_steps", LINKS_POOL)
        lam_ready = signal("lambda_abs_ready", 1)
        lam_exp = signal("lambda_exp_ready", 1)
        dc_ready = signal("derived_ready", 1)
        xc_ready = signal("conv_ready", 1)
        rg_done = signal("recurrent_gate_done", 6)
        rg_ready = signal("recurrent_gate_ready", 6)
        ab_ready = signal("decay_ready", 2)
        bb_ready = signal("one_minus_a2_ready", 1)
        bs_ready = signal("branch_input_scale_ready", 1)
        ge_in = signal("gelu_argument_ready", 1)
        ge_out = signal("gelu_gate_ready", 1)
        b_done = signal("branch_done", 1)
        tm_done = signal("transposed", 11)
        tm_ready = signal("token_major_ready", 11)
        fb_ready = signal("forget_abs_ready", 1)
        fe_ready = signal("forget_log_ready", 1)
        row_ready = signal("gate_rows_ready", 2)
        gc_done = signal("g_column_done", 1)
        gc_ready = signal("g_column_ready", 1)
        wb_done = signal("spread_done", 4)
        wb_ready = signal("spread_ready", 4)
        qw_ready = signal("q_weighted_ready", 1)
        gb_done = signal("g_spread_done", 5)
        we_ready = signal("weight_exp_ready", 5)
        wm_ready = signal("weight_masked_ready", 5)
        sc_done = signal("qk_done", 5)
        at_ready = signal("a_ready", 5)
        kw_ready = signal("k_weighted_ready", 5)
        nd_done = signal("num_den_done", 5)
        hc_ready = signal("memory_read_ready", 5)
        cu_done = signal("memory_update_done", 4 + NB)
        cu_ready = signal("memory_ready", 4 + NB)
        oc_ready = signal("output_gate_ready", 1)
        c_done = signal("memory_group_done", 1)
        s_done = signal("scores_done", 24)
        mx_ready = signal("row_max_ready", 26)
        e_ready = signal("exp_ready", 26)
        p_done = signal("probs_ready", 26)
        pt_done = signal("probs_transposed", 24 + 4)
        pt_ready = signal("probs_token_major", 24 + 4)
        o_done = signal("attention_out_done", 24)
        o_ready = signal("attention_out_ready", 24 + 2)
        q_ready = signal("q_blocks_ready", 1)
        qz_ready = signal("q_blocks_zeroed", 1)
        kv_used = signal("kv_used", 16)
        gs_ready = signal("group_square_ready", 8)
        gst_done = signal("group_mean_done", 4)
        gr_ready = signal("group_rstd_ready", 4)

        block = ctx.enter_context(nc.Block())

        @block.sync
        def _(sy):
            sy.dma_start(con[:, :], consts).then_inc(const_loaded.sem, 16)
            for k in range(2):
                sy.dma_start(raw[:, k, :], weights[k]).then_inc(loaded[k].sem, 16)
            sy.dma_start(x[:], x_in).then_inc(x_loaded.sem, 16)
            with sy.Fori(0, DEPTH) as L:
                def chunks(first, count):
                    with sy.Fori(0, count // 2) as f:
                        for k in range(2):
                            sy.wait_ge(lo.sem, lo.at(L, first + k + 1) + f * 2)
                            sy.dma_start(raw[:, k, :], weights[L * CHUNKS + f * 2 + (first + k + 2)]) \
                              .then_inc(loaded[k].sem, 16)

                sy.wait_ge(layer_done.sem, L + 1)
                sy.dma_start(pc[:, :], par[L]).then_inc(par_loaded.sem, 16)
                sy.dma_start(rg[:], rgw[L]).then_inc(par_loaded.sem, 16)
                chunks(CH_F1, CH_OUT + 2 - CH_F1)
                sy.wait_ge(z_done.sem, z_done.at(L, NZ))
                sy.dma_start(xs[:, :, :, 0:3], I["sconv"][L]).then_inc(sb_loaded.sem, 16)
                sy.dma_start(h0[:], I["sh"][L]).then_inc(sb_loaded.sem, 16)
                sy.dma_start(cs[:], I["sc"][L]).then_inc(sc_loaded.sem, 16)
                sy.wait_ge(z_ready.sem, z_ready.at(L, NZ))
                sy.dma_start(O["k"][L], z[:, ZK:ZK + 3, :]).then_inc(z_stored.sem, 16)
                sy.dma_start(O["v"][L], z[:, ZV:ZV + 3, :]).then_inc(z_stored.sem, 16)
                sy.wait_ge(b_done.sem, b_done.at(L, 1))
                sy.dma_start(O["sb"][L], sb_[:, :]).then_inc(sb_stored.sem, 16)
                sy.wait_ge(sb_stored.sem, sb_stored.at(L, 1))
                sy.dma_start(m0[:], I["sm"][L]).then_inc(sc_loaded.sem, 16)
                sy.wait_ge(c_done.sem, c_done.at(L, 1))
                sy.dma_start(O["cp"][L], cp[:]).then_inc(sc_stored.sem, 16)
                sy.dma_start(O["cs"][L], cs[:]).then_inc(sc_stored.sem, 16)
                sy.dma_start(O["m"][L], mo[:]).then_inc(sc_stored.sem, 16)
                sy.wait_ge(sc_stored.sem, sc_stored.at(L, 3))
                for n in range(16):
                    g, what, j = n // 8, n % 8 // 4, n % 4
                    if n >= 4:
                        sy.wait_ge(kv_used.sem, kv_used.at(L, n - 3))
                    sy.dma_start(kv[:, n % 4, :], (I["kc"] if what == 0 else I["vc"])[L, 4 * g + j]) \
                      .then_inc(kv_loaded[n % 4].sem, 16)
                chunks(CH_OUT + 2, CH_D2 - CH_OUT - 2)
                chunks(CH_D2, C_DOWN)
                sy.wait_ge(out_done.sem, out_done.at(L, 3 * KT))
                sy.dma_start(pe_raw[:], pe_in[L]).then_inc(pe_loaded.sem, 16)
                chunks(CH_PJ, C_PJ + C_PG)
            sy.wait_ge(layer_done.sem, DEPTH + 1)
            sy.dma_start(O["x"], x[:]).then_inc(x_stored.sem, 16)
            sy.wait_ge(x_stored.sem, 16)
            sy.wait_ge(z_stored.sem, 16 * 2 * DEPTH)
            sy.wait_ge(sb_stored.sem, 16 * DEPTH)
            sy.wait_ge(sc_stored.sem, 16 * 3 * DEPTH)
            sy.wait_ge(loaded[0].sem, 16 * (CHUNKS // 2 * DEPTH + 1))
            sy.wait_ge(loaded[1].sem, 16 * (CHUNKS // 2 * DEPTH + 1))

        @block.tensor
        def _(pe):
            def mean_square(L, n):
                pe.wait_ge(sq_added.sem, sq_added.at(L, 7 * n))
                for h in range(2):
                    ins = pe.matmul(T(0)[:, h, :], ones, acc[:, h, :], start=True, stop=True)
                ins.then_inc(stat_done.sem, 1)

            def block3(out, slot, b, rh, rl, first, last):
                w_h, w_l = wh[:, slot, b * P:(b + 1) * P], wl[:, slot, b * P:(b + 1) * P]
                for n, (w, r) in enumerate(((w_h, rh), (w_h, rl), (w_l, rh))):
                    for h in range(2):
                        ins = pe.matmul(out[:, h, :], w, r[:, h, :], start=first and n == 0,
                                        stop=last and n == 2)
                return ins

            def gate_up(L, s):
                pre = (N_F1, N_F2)[s]
                c0 = (CH_F1, CH_F2)[s]
                with pe.Fori(0, FT // 2) as f:
                    for j in range(2):
                        pe.wait_ge(h_ready.sem, h_ready.at(L, s * FT + j - 1) + f * 2)
                        pe.wait_ge(lo.sem, lo.at(L, c0 + 2 * j + 1) + f * 4)
                        for k in range(KT):
                            pe.wait_ge(nl_ready.sem, nl_ready.at(L, pre * KT + k + 1))
                            ins = block3(T(2 * j), 0, k, xh[:, k], xl[:, k], k == 0, k == KT - 1)
                        ins.then_inc(gate_done.sem, 1)
                        pe.wait_ge(lo.sem, lo.at(L, c0 + 2 * j + 2) + f * 4)
                        for k in range(KT):
                            ins = block3(T(2 * j + 1), 1, k, xh[:, k], xl[:, k], k == 0, k == KT - 1)
                        ins.then_inc(up_done.sem, 1)

            def out_tiles(L, first, c0, ff):
                per = 3 if ff else 1
                with pe.Fori(0, 2) as f:
                    for j in range(4):
                        pe.wait_ge(y_ready.sem, y_ready.at(L, first + j - 3) + f * 4)
                        k = 0
                        for p in range(per):
                            c = j * per + p
                            pe.wait_ge(lo.sem, lo.at(L, c0 + c + 1) + f * (4 * per))
                            for b in range(DOWN_BLOCKS[p] if ff else KT):
                                rh, rl = (hh, hl) if ff else (xh, xl)
                                last = b == (DOWN_BLOCKS[p] if ff else KT) - 1
                                ins = block3(T(j), c % 2, b, rh[:, k], rl[:, k], k == 0,
                                             p == per - 1 and last)
                                k += 1
                            if p < per - 1:
                                ins.then_inc(part_used.sem, 1)
                        ins.then_inc(out_done.sem, 1)

            def mix_tensor(pe, L):
                unit = 0
                for t in range(4):
                    cols = slice(t * P, (t + 1) * P)
                    for tiles in ((ZV, ZV + 1, ZV + 2), (ZKC, ZKC + 1, ZVC, ZVC + 1)):
                        if unit >= 4:
                            pe.wait_ge(tm_ready.sem, tm_ready.at(L, unit - 3))
                        for n, k in enumerate(tiles):
                            ins = pe.transpose(psum[:, 4 + unit % 4, n * P:(n + 1) * P], z[:, k, cols], ident)
                        ins.then_inc(tm_done.sem, 1)
                        unit += 1
                for g in range(2):
                    pe.wait_ge(tm_ready.sem, tm_ready.at(L, unit - 3))
                    for n in range(3):
                        ins = pe.transpose(psum[0:KEYS_NEW, 4 + unit % 4, n * P:(n + 1) * P],
                                           z[:, ZV + n, SEQ + KEYS_NEW * g:SEQ + KEYS_NEW * (g + 1)], ident)
                    ins.then_inc(tm_done.sem, 1)
                    unit += 1
                pe.wait_ge(tm_ready.sem, tm_ready.at(L, unit - 3))
                for n, k in enumerate((ZKC, ZKC + 1, ZVC, ZVC + 1)):
                    ins = pe.transpose(psum[0:32, 4 + unit % 4, n * P:(n + 1) * P], z[:, k, SEQ:TOK], ident)
                ins.then_inc(tm_done.sem, 1)
                pe.wait_ge(tm_ready.sem, tm_ready.at(L, 11))

                pe.wait_ge(par_loaded.sem, par_loaded.at(L, 2))
                pe.wait_ge(xc_ready.sem, xc_ready.at(L, 1))
                for j in range(3):
                    for i in range(2):
                        if j == 2:
                            pe.wait_ge(rg_ready.sem, rg_ready.at(L, i + 1))
                        t = T(2 * (j % 2) + i)
                        for h in range(2):
                            ins = pe.matmul(t[:, h, :], rg[:, i, j, :], xc[:, j, h * HALF:(h + 1) * HALF],
                                            start=True, stop=True)
                        ins.then_inc(rg_done.sem, 1)

                pe.wait_ge(rg_ready.sem, rg_ready.at(L, 6))
                pe.wait_ge(row_ready.sem, row_ready.at(L, 1))
                pe.nop(nofuse=True)
                for t in range(5):
                    n = P if t < 4 else 32
                    ins = pe.transpose(psum[0:n, 4, t * HC:(t + 1) * HC], rows[:, GR, t * P:t * P + n],
                                       ident[0:HC, 0:HC])
                ins.then_inc(gc_done.sem, 1)
                pe.wait_ge(gc_ready.sem, gc_ready.at(L, 1))
                pe.wait_ge(row_ready.sem, row_ready.at(L, 2))
                for w, row in enumerate((DW, MT)):
                    for c in range(2):
                        t = T(2 * w + c)
                        for h in range(2):
                            ins = pe.matmul(t[:, h, :], con[0:HC, K_SEL2 + c * P:K_SEL2 + (c + 1) * P],
                                            rows[:, row, h * HALF:(h + 1) * HALF], start=True, stop=True)
                        ins.then_inc(wb_done.sem, 1)
                pe.wait_ge(wb_ready.sem, wb_ready.at(L, 4))

                def spread_g(t):
                    n = P if t < 4 else 32
                    if t >= 2:
                        pe.wait_ge(we_ready.sem, we_ready.at(L, t - 1))
                    for h in range(HC):
                        ins = pe.matmul(psum[:, t % 2, h * P:h * P + n],
                                        con[0:HC, K_SELH + h * P:K_SELH + (h + 1) * P],
                                        rows[:, GG, t * P:t * P + n], start=True, stop=True)
                    ins.then_inc(gb_done.sem, 1)

                def qk(t):
                    n = P if t < 4 else 32
                    if t >= 2:
                        pe.wait_ge(at_ready.sem, at_ready.at(L, t - 1))
                        pe.nop(nofuse=True)
                    for h in (0, 2, 1, 3):
                        r = slice(HD * (h % 2), HD * (h % 2) + HD)
                        if h == 1:
                            steps.link(ins, hold=True)
                        ins = pe.matmul(psum[0:n, 2 + t % 2, h * P:h * P + n], z[r, ZKC + h // 2, t * P:t * P + n],
                                        z[r, ZQC + h // 2, t * P:t * P + n], start=True, stop=True)
                    ins.then_inc(sc_done.sem, 1)

                def read(t):
                    n = P if t < 4 else 32
                    if t >= 2:
                        pe.wait_ge(hc_ready.sem, hc_ready.at(L, t - 1))
                    pe.wait_ge(at_ready.sem, at_ready.at(L, t + 1))
                    if t == 1:
                        pe.wait_ge(qw_ready.sem, qw_ready.at(L, 1))
                    if 1 <= t < 4:
                        pe.wait_ge(cu_ready.sem, cu_ready.at(L, t))
                    for p in range(2):
                        if p and t:
                            steps.link(ins)
                        for c in range(2):
                            h, r = 2 * c + p, slice(HD * p, HD * p + HD)
                            for den in range(2):
                                o = psum[r, 4 + t % 2, den * 256 + c * P:den * 256 + c * P + n]
                                w = va[0:n, t, h, 0:HD] if not den else con[0:n, K_ONE:K_ONE + HD]
                                ins = pe.matmul(o, w, at_[0:n, h, 0:n], start=True, stop=(t == 0))
                                if 1 <= t < 4:
                                    w = cp[r, c, 0:HD] if not den else cp[r, c, HD:HD + 1].to_broadcast([HD, HD])
                                    ins = pe.matmul(o, w, qw[r, c, t * P:t * P + n], start=False, stop=True)
                                if t == 4:
                                    for b in range(NB):
                                        w = (cs[r, b, c, 0:HD] if not den
                                             else cs[r, b, c, HD:HD + 1].to_broadcast([HD, HD]))
                                        k = den * 256 + c * P + NT * b
                                        ins = pe.matmul(psum[r, 4 + t % 2, k:k + NT], w,
                                                        qw[r, c, SEQ + NT * b:SEQ + NT * b + NT],
                                                        start=False, stop=(b == NB - 1))
                    ins.then_inc(nd_done.sem, 1)

                def update(t):
                    pe.wait_ge(kw_ready.sem, kw_ready.at(L, t + 1))
                    if t < 4:
                        if t >= 2:
                            pe.wait_ge(cu_ready.sem, cu_ready.at(L, t - 1))
                        for c in range(2):
                            ins = pe.matmul(psum[:, 6 + t % 2, c * 130:(c + 1) * 130], kw[:, 2 * c:2 * c + 2, :],
                                            va[:, t, 2 * c:2 * c + 2, :], start=True, stop=True)
                        ins.then_inc(cu_done.sem, 1)
                    else:
                        for b in range(NB):
                            pe.wait_ge(cu_ready.sem, cu_ready.at(L, 4 + b - 1))
                            for c in range(2):
                                ins = pe.matmul(psum[:, 6 + b % 2, c * 130:(c + 1) * 130],
                                                kwm[:, b, 2 * c:2 * c + 2, :], va[0:32, 4, 2 * c:2 * c + 2, :],
                                                start=True, stop=True)
                            ins.then_inc(cu_done.sem, 1)

                spread_g(0)
                qk(0)
                for t in range(5):
                    if t < 4:
                        spread_g(t + 1)
                        qk(t + 1)
                    read(t)
                    update(t)
                pe.wait_ge(hc_ready.sem, hc_ready.at(L, 5))
                pe.wait_ge(cu_ready.sem, cu_ready.at(L, 4 + NB))

                def scores(u):
                    h, qb = u // 4, u % 4
                    r, n = slice(HD * (h % 2), HD * (h % 2) + HD), (qb + 1) * P
                    if u >= 4:
                        pe.wait_ge(mx_ready.sem, mx_ready.at(L, u - 3))
                    pe.matmul(psum[:, u % 4, 0:n], z[r, ZQ + h // 2, qb * P:(qb + 1) * P],
                              z[r, ZK + h // 2, 0:n], start=True, stop=True).then_inc(s_done.sem, 1)

                def turn(u):
                    pe.wait_ge(p_done.sem, p_done.at(L, u + 1))
                    if u >= 2:
                        pe.wait_ge(pt_ready.sem, pt_ready.at(L, u - 1))
                    for kb in range(u % 4 + 1):
                        ins = pe.transpose(psum[:, 4 + u % 2, kb * P:(kb + 1) * P],
                                           pp[:, u % 2, kb * P:(kb + 1) * P], ident)
                    ins.then_inc(pt_done.sem, 1)

                def values(u):
                    h, qb = u // 4, u % 4
                    r = slice(HD * (h % 2), HD * (h % 2) + HD)
                    pe.wait_ge(pt_ready.sem, pt_ready.at(L, u + 1))
                    if u >= 2:
                        pe.wait_ge(o_ready.sem, o_ready.at(L, u - 1))
                    for kb in range(qb + 1):
                        ins = pe.matmul(psum[r, 6 + u % 2, 0:P], vt[:, kb, h * HD:(h + 1) * HD],
                                        ptp[:, u % 2, kb, :], start=(kb == 0), stop=(kb == qb))
                    ins.then_inc(o_done.sem, 1)

                for i in range(24 + 3):
                    if i < 24:
                        scores(i)
                    if 2 <= i < 26:
                        turn(i - 2)
                    if i >= 3:
                        values(i - 3)

                pe.wait_ge(q_ready.sem, q_ready.at(L, 1))
                cut = KS // 2
                for g in range(2):
                    pe.wait_ge(mx_ready.sem, mx_ready.at(L, 24 + g))
                    for j in range(4):
                        b = 4 * g + j
                        pe.wait_ge(kv_loaded[j].sem, kv_loaded[j].at(L, 2 * g + 1))
                        rr = slice(32 * j, 32 * j + 32)
                        k_t = kv[:, j, 0:3 * KEYS].rearrange("p (c n) -> p c n", c=3)
                        for o0, n, src in ((0, cut, k_t[:, :, 0:cut]), (512, KEYS - cut, k_t[:, :, cut:KEYS]),
                                           (512 + KEYS - cut, KEYS_NEW,
                                            z[:, ZK:ZK + 3, SEQ + KEYS_NEW * g:SEQ + KEYS_NEW * (g + 1)])):
                            for c in range(3):
                                ins = pe.matmul(psum[rr, 2 * g + o0 // 512, o0 % 512:o0 % 512 + n], qbd[:, b, c, :],
                                                src[:, c, :], start=(c == 0), stop=(c == 2))
                        ins.then_inc(kv_used.sem, 1)
                    pe.wait_ge(p_done.sem, p_done.at(L, 25 + g))
                    pe.wait_ge(pt_ready.sem, pt_ready.at(L, 24 + 2 * g))
                    for q in range(2):
                        for kb in range(4 * q, 4 * q + 4):
                            n = P if kb < 7 else KEYS_NEW
                            ins = pe.transpose(psum[0:n, 4 + q, kb % 4 * P:(kb % 4 + 1) * P],
                                               ps_[:, kb * P:kb * P + n], ident)
                        ins.then_inc(pt_done.sem, 1)
                    pe.wait_ge(pt_ready.sem, pt_ready.at(L, 26 + 2 * g))
                    pe.wait_ge(o_ready.sem, o_ready.at(L, 24 + g))
                    for j in range(4):
                        pe.wait_ge(kv_loaded[j].sem, kv_loaded[j].at(L, 2 * g + 2))
                        for c in range(3):
                            o = psum[:, 6 + g, (j * 3 + c) * 8:(j * 3 + c) * 8 + 8]
                            q = slice(32 * j + 8 * c, 32 * j + 8 * c + 8)
                            for kb in range(7):
                                pe.matmul(o, kv[:, j, kb * 384 + c * P:kb * 384 + (c + 1) * P], pts[:, kb, q],
                                          start=(kb == 0), stop=False)
                            ins = pe.matmul(o, vs[:, g, c * P:(c + 1) * P], pts[0:KEYS_NEW, 7, q],
                                            start=False, stop=True)
                        ins.then_inc(kv_used.sem, 1)
                pe.wait_ge(o_ready.sem, o_ready.at(L, 26))

                first = 0
                for n, tiles in enumerate((3, 3, 1, 1)):
                    for k in range(tiles):
                        pe.wait_ge(gs_ready.sem, gs_ready.at(L, first + 1))
                        for h in range(2):
                            ins = pe.matmul(T(n)[:, h, :], ones if n < 2 else blk, y_ff[:, first, h, :],
                                            start=(k == 0), stop=(k == tiles - 1))
                        first += 1
                    ins.then_inc(gst_done.sem, 1)

            pe.wait_ge(const_loaded.sem, 16)
            with pe.Fori(0, DEPTH) as L:
                steps = Steps(pe, pe_steps, L)
                mean_square(L, 0)
                gate_up(L, 0)
                pe.wait_ge(hl_ready.sem, hl_ready.at(L, FT))
                pe.nop(nofuse=True)
                out_tiles(L, 0, CH_D1, True)
                mean_square(L, 1)
                mean_square(L, 2)
                with pe.Fori(0, NZ // 4) as f:
                    for j in range(4):
                        pe.wait_ge(z_ready.sem, z_ready.at(L, j - 1) + f * 4)
                        pe.wait_ge(lo.sem, lo.at(L, CH_IN + j + 1) + f * 4)
                        for k in range(KT):
                            pe.wait_ge(nl_ready.sem, nl_ready.at(L, N_MIX * KT + k + 1))
                            ins = block3(T(j % 2), j % 2, k, xh[:, k], xl[:, k], k == 0, k == KT - 1)
                        ins.then_inc(z_done.sem, 1)
                pe.wait_ge(z_ready.sem, z_ready.at(L, NZ))
                mix_tensor(pe, L)
                pe.wait_ge(nl_ready.sem, nl_ready.at(L, (N_OUT + 1) * KT))
                pe.nop(nofuse=True)
                out_tiles(L, KT, CH_OUT, False)
                mean_square(L, 3)
                mean_square(L, 4)
                gate_up(L, 1)
                pe.wait_ge(hl_ready.sem, hl_ready.at(L, 2 * FT))
                pe.nop(nofuse=True)
                out_tiles(L, 2 * KT, CH_D2, True)
                mean_square(L, 5)
                pe.wait_ge(p_ready.sem, p_ready.at(L, 2))
                pe.wait_ge(rstd_ready.sem, rstd_ready.at(L, 6))
                for d in range(KT):
                    if d % 4 == 0:
                        pe.wait_ge(lo.sem, lo.at(L, CH_PJ + d // 4 + 1))
                    if d == 4:
                        pe.wait_ge(pj_ready.sem, pj_ready.at(L, 4))
                        mean_square(L, 6)
                        pe.wait_ge(rstd_ready.sem, rstd_ready.at(L, 7))
                    for k in range(2):
                        ins = block3(T(d % 4), d // 4, d % 4 * 2 + k, ph[:, k], pl[:, k], k == 0, k == 1)
                    ins.then_inc(pj_done.sem, 1)
                pe.wait_ge(pj_ready.sem, pj_ready.at(L, KT))
                pe.nop(nofuse=True)
                with pe.Fori(0, KT // 2) as f:
                    for j in range(2):
                        pe.wait_ge(pg_ready.sem, pg_ready.at(L, j - 1) + f * 2)
                        pe.wait_ge(lo.sem, lo.at(L, CH_PG + j + 1) + f * 2)
                        for k in range(KT):
                            pe.wait_ge(nl_ready.sem, nl_ready.at(L, N_PLE * KT + k + 1))
                            ins = block3(T(j), j, k, xh[:, k], xl[:, k], k == 0, k == KT - 1)
                        ins.then_inc(pg_done.sem, 1)
                pe.wait_ge(pg_ready.sem, pg_ready.at(L, KT))
                mean_square(L, 7)
                steps.end()

        @block.scalar
        def _(act):
            def split(slot, loads):
                act.wait_ge(loaded[slot].sem, loads)
                act.copy(wh[:, slot, :], raw[:, slot, :]).then_inc(hi.sem, 1)

            def loads(L, c, f=None, per=0):
                n = loaded[0].at(L, (c + 2) // 2 + 1)
                return n if f is None else n + f * (8 * per)

            def square(L, n, k, src):
                act.wait_ge(sq_added.sem, sq_added.at(L, 7 * n + (0 if k < 2 else max(k - 2, 1))))
                act.activation(sq[:, k % 2], src, ACT.Square).then_inc(sq_ready.sem, 1)

            def inverse_rms(L, n):
                act.wait_ge(stat_done.sem, stat_done.at(L, n + 1))
                steps.link(act.activation(rstd[:], T(0), ACT.Ln, bias=EPS, scale=1.0 / D))
                act.activation(rstd[:], rstd[:], ACT.Exp, scale=-0.5).then_inc(rstd_ready.sem, 1)

            def x_squares(L, m):
                for k in range(KT):
                    act.wait_ge(xn_ready.sem, xn_ready.at(L, m * KT + k + 1))
                    square(L, 2 * m + 1, k, x[:, k])

            def normed_hi(L, q):
                for k in range(KT):
                    act.wait_ge(n_ready.sem, n_ready.at(L, q * KT + k + 1))
                    act.copy(xh[:, k], tmp[:, k % 2]).then_inc(nh_ready.sem, 1)

            def gate_up(L, s):
                c0 = (CH_F1, CH_F2)[s]
                act.preload_act_table(ACT.Silu)
                with act.Fori(0, FT // 2) as f:
                    for j in range(2):
                        t = s * FT + j
                        act.wait_ge(gate_done.sem, gate_done.at(L, t + 1) + f * 2)
                        act.wait_ge(hl_ready.sem, hl_ready.at(L, t - 1) + f * 2)
                        act.activation(act_out[:, j], T(2 * j), ACT.Silu).then_inc(silu_ready.sem, 1)
                        split(0, loads(L, c0 + 2 * j, f, 4))
                        act.wait_ge(up_done.sem, up_done.at(L, t + 1) + f * 2)
                        split(1, loads(L, c0 + 2 * j + 1, f, 4))
                        act.wait_ge(h_ready.sem, h_ready.at(L, t + 1) + f * 2)
                        act.copy(hh[:, bass.ds(f * 2 + j, 1)], act_out[:, j:j + 1]).then_inc(hh_ready.sem, 1)

            def out_tiles(L, first, c0, s, n, y):
                per = 1 if s is None else 3
                for d in range(KT):
                    for p in range(per):
                        c = d * per + p
                        if p < per - 1:
                            act.wait_ge(part_used.sem, part_used.at(L, 2 * (s * KT + d) + p + 1))
                        else:
                            act.wait_ge(out_done.sem, out_done.at(L, first + d + 1))
                        split(c % 2, loads(L, c0 + c))
                    act.wait_ge(y_ready.sem, y_ready.at(L, first + d + 1))
                    square(L, n, d, y[:, d])

            def mix_scalar(L):
                act.wait_ge(z_done.sem, z_done.at(L, NZ))
                for u in range(11):
                    b = 4 + u % 4
                    act.wait_ge(tm_done.sem, tm_done.at(L, u + 1))
                    if u < 8 and u % 2 == 0:
                        act.copy(vt[:, u // 2, :], psum[:, b, 0:384]).then_inc(tm_ready.sem, 1)
                    elif u in (8, 9):
                        act.copy(vs[:, u - 8, :], psum[0:KEYS_NEW, b, 0:384]).then_inc(tm_ready.sem, 1)
                    else:
                        t, r = (u // 2, slice(0, P)) if u < 8 else (4, slice(0, 32))
                        act.mul(kc[r, t, :], psum[r, b, 0:256], SCALE)
                        act.copy(va[r, t, :, 0:HD],
                                 psum[r, b, 256:512].rearrange("p (h d) -> p h d", h=HC)).then_inc(tm_ready.sem, 1)
                for j in range(3):
                    for i in range(2):
                        act.wait_ge(rg_done.sem, rg_done.at(L, 2 * j + i + 1))
                        b_ = pc[:, (B_RA, B_RX)[i] + j:(B_RA, B_RX)[i] + j + 1]
                        act.activation(gt[:, j, i, :].rearrange("p (h n) -> p h n", h=2), T(2 * (j % 2) + i),
                                       ACT.Sigmoid, bias=b_).then_inc(rg_ready.sem, 1)
                act.wait_ge(ge_in.sem, ge_in.at(L, 1))
                act.activation(ge[:], ge[:], ACT.Sigmoid).then_inc(ge_out.sem, 1)
                act.activation(z[:, ZOC:ZOC + 2, :], z[:, ZOC:ZOC + 2, :], ACT.Sigmoid).then_inc(oc_ready.sem, 1)
                act.wait_ge(dc_ready.sem, dc_ready.at(L, 1))
                act.wait_ge(rg_ready.sem, rg_ready.at(L, 6))
                for j in range(3):
                    ins = act.activation(bv[:, j, :], gt[:, j, 0, :], ACT.Tanh,
                                         scale=dc[:, D_SPPOS + j:D_SPPOS + j + 1])
                ins.then_inc(ab_ready.sem, 1)
                for j in range(3):
                    ins = act.activation(av[:, j, :], gt[:, j, 0, :], ACT.Exp,
                                         scale=dc[:, D_SPNEG + j:D_SPNEG + j + 1])
                ins.then_inc(ab_ready.sem, 1)
                act.wait_ge(bb_ready.sem, bb_ready.at(L, 1))
                act.activation(bv[:], gt[:, :, 0, :], ACT.Sqrt).then_inc(bs_ready.sem, 1)

                act.preload_act_table_set(EXP_LN)
                act.wait_ge(fb_ready.sem, fb_ready.at(L, 1))
                steps.link(act.activation(rows[:, DW, :], rows[:, DW, :], ACT.Exp, scale=-1.0))
                act.activation(rows[:, DW, :], rows[:, DW, :], ACT.Ln, bias=1.0).then_inc(fe_ready.sem, 1)
                for w, dst in enumerate((wi, em)):
                    for c in range(2):
                        act.wait_ge(wb_done.sem, wb_done.at(L, 2 * w + c + 1))
                        act.activation(dst[:, c, :].rearrange("p (h n) -> p h n", h=2), T(2 * w + c), ACT.Exp,
                                       scale=(1.0, -1.0)[w]).then_inc(wb_ready.sem, 1)
                act.wait_ge(gc_ready.sem, gc_ready.at(L, 1))
                for t in range(5):
                    n = P if t < 4 else 32
                    act.wait_ge(gb_done.sem, gb_done.at(L, t + 1))
                    if t:
                        act.wait_ge(kw_ready.sem, kw_ready.at(L, t))
                    for h in range(HC):
                        ins = act.activation(wt[0:n, h, 0:n], psum[0:n, t % 2, h * P:h * P + n], ACT.Exp,
                                             scale=-1.0, bias=gc[0:n, t, h:h + 1])
                    ins.then_inc(we_ready.sem, 1)

                for i in range(24 + 2):
                    if i < 24:
                        act.wait_ge(mx_ready.sem, mx_ready.at(L, i + 1))
                        n = (i % 4 + 1) * P
                        act.activation(pp[:, i % 2, 0:n], pp[:, i % 2, 0:n], ACT.Exp, scale=SCALE,
                                       bias=stat[:, i % 2, 1:2]).then_inc(e_ready.sem, 1)
                    if i >= 2:
                        u = i - 2
                        n = (u % 4 + 1)
                        act.wait_ge(pt_done.sem, pt_done.at(L, u + 1))
                        if u >= 2:
                            act.wait_ge(o_done.sem, o_done.at(L, u - 1))
                        act.copy(ptp[:, u % 2, 0:n, :],
                                 psum[:, 4 + u % 2, 0:n * P].rearrange("p (k n) -> p k n", n=P)) \
                           .then_inc(pt_ready.sem, 1)
                for g in range(2):
                    act.wait_ge(mx_ready.sem, mx_ready.at(L, 25 + g))
                    act.activation(ps_[:, :], ps_[:, :], ACT.Exp, scale=SCALE,
                                   bias=stat[:, g, 1:2]).then_inc(e_ready.sem, 1)
                    for q in range(2):
                        act.wait_ge(pt_done.sem, pt_done.at(L, 24 + 2 * g + q + 1))
                        if g:
                            act.wait_ge(kv_used.sem, kv_used.at(L, 8))
                        src = psum[:, 4 + q, :].rearrange("p (k n) -> p k n", n=P)
                        if q == 0:
                            act.copy(pts[:, 0:4, :], src).then_inc(pt_ready.sem, 1)
                        else:
                            act.copy(pts[:, 4:7, :], src[:, 0:3, :])
                            act.copy(pts[0:KEYS_NEW, 7, :], src[0:KEYS_NEW, 3, :]).then_inc(pt_ready.sem, 1)

                act.wait_ge(o_ready.sem, o_ready.at(L, 26))
                act.wait_ge(sc_stored.sem, sc_stored.at(L, 3))
                for k, src in enumerate(OUT_TILES):
                    act.activation(y_ff[:, k].rearrange("p h n -> p (h n)"), z[:, src, :], ACT.Square) \
                       .then_inc(gs_ready.sem, 1)
                for n in range(4):
                    act.wait_ge(gst_done.sem, gst_done.at(L, n + 1))
                    steps.link(act.activation(gr[:, n], T(n), ACT.Ln, bias=EPS,
                                              scale=1.0 / (DB if n < 2 else HD)))
                    act.activation(gr[:, n], gr[:, n], ACT.Exp, scale=-0.5).then_inc(gr_ready.sem, 1)

            split(0, 16)
            split(1, 16)
            act.wait_ge(x_loaded.sem, 16)
            for k in range(KT):
                if k >= 2:
                    act.wait_ge(sq_added.sem, max(k - 2, 1))
                act.activation(sq[:, k % 2], x[:, k], ACT.Square).then_inc(sq_ready.sem, 1)
            act.preload_act_table_set(EXP_LN)
            with act.Fori(0, DEPTH) as L:
                steps = Steps(act, act_steps, L)
                act.wait_ge(lam_ready.sem, lam_ready.at(L, 1))
                act.activation(sp[:, 1, :], sp[:, 0, :], ACT.Exp, scale=-1.0).then_inc(lam_exp.sem, 1)
                inverse_rms(L, 0)
                normed_hi(L, N_F1)
                gate_up(L, 0)
                out_tiles(L, 0, CH_D1, 0, 0, y_ff)
                act.preload_act_table_set(EXP_LN)
                inverse_rms(L, 1)
                x_squares(L, 0)
                inverse_rms(L, 2)
                normed_hi(L, N_MIX)
                with act.Fori(0, NZ // 4) as f:
                    for j in range(4):
                        act.wait_ge(z_done.sem, z_done.at(L, j + 1) + f * 4)
                        split(j % 2, loads(L, CH_IN + j, f, 4))
                        act.copy(z[:, bass.ds(f * 4 + j, 1), :].rearrange("p k (h n) -> p (k h) n", h=2),
                                 T(j % 2)).then_inc(z_ready.sem, 1)
                mix_scalar(L)
                normed_hi(L, N_OUT)
                out_tiles(L, KT, CH_OUT, None, 2, y_z)
                inverse_rms(L, 3)
                x_squares(L, 1)
                inverse_rms(L, 4)
                normed_hi(L, N_F2)
                gate_up(L, 1)
                out_tiles(L, 2 * KT, CH_D2, 1, 4, y_ff)
                act.wait_ge(pe_loaded.sem, pe_loaded.at(L, 1))
                act.copy(ph[:], pe_raw[:]).then_inc(p_ready.sem, 1)
                act.preload_act_table_set(EXP_LN)
                inverse_rms(L, 5)
                act.wait_ge(pj_done.sem, pj_done.at(L, 4))
                split(0, loads(L, CH_PJ))
                x_squares(L, 2)
                inverse_rms(L, 6)
                normed_hi(L, N_PLE)
                act.wait_ge(pj_done.sem, pj_done.at(L, KT))
                split(1, loads(L, CH_PJ + 1))
                act.preload_act_table(ACT.Sigmoid)
                for d in range(KT):
                    act.wait_ge(pg_done.sem, pg_done.at(L, d + 1))
                    split(d % 2, loads(L, CH_PG + d))
                    act.wait_ge(ye_ready.sem, ye_ready.at(L, d - 1))
                    act.activation(act_out[:, d % 2], T(d % 2), ACT.Sigmoid).then_inc(pg_ready.sem, 1)
                    act.wait_ge(ye_ready.sem, ye_ready.at(L, d + 1))
                    square(L, 6, d, y_z[:, d])
                act.preload_act_table_set(EXP_LN)
                inverse_rms(L, 7)
                x_squares(L, 3)
                steps.end()

        @block.vector
        def _(ve):
            def add_square(L, n, i):
                ve.wait_ge(sq_ready.sem, sq_ready.at(L, 8 * n + i + 1))
                if i == 1:
                    ve.wait_ge(stat_done.sem, stat_done.at(L, n + 1))
                    a = sq[:, 0]
                else:
                    ve.wait_ge(sq_added.sem, sq_added.at(L, 7 * n + i - 1))
                    a = acc[:]
                ve.tensor_tensor(acc[:], a, sq[:, i % 2], ALU.add).then_inc(sq_added.sem, 1)

            def add_norm(L, m, n, y, g):
                ve.wait_ge(rstd_ready.sem, rstd_ready.at(L, n + 1))
                for k in range(KT):
                    steps.link(ve.scalar_tensor_tensor(tmp[:, k % 2], y[:, k], g[:, k:k + 1], rstd[:],
                                                       ALU.mult, ALU.mult))
                    ve.tensor_tensor(x[:, k], x[:, k], tmp[:, k % 2], ALU.add).then_inc(xn_ready.sem, 1)
                    if k >= 2:
                        add_square(L, 2 * m + 1, k - 1)
                add_square(L, 2 * m + 1, KT - 1)

            def normed(L, q, src, g, inv):
                def lo_part(k):
                    ve.wait_ge(nh_ready.sem, nh_ready.at(L, q * KT + k + 1))
                    ve.tensor_tensor(xl[:, k], tmp[:, k % 2], xh[:, k].bitcast(F32), ALU.subtract) \
                      .then_inc(nl_ready.sem, 1)
                for k in range(KT):
                    if k >= 2:
                        ve.wait_ge(nl_ready.sem, nl_ready.at(L, q * KT + k - 1))
                    ve.scalar_tensor_tensor(tmp[:, k % 2], src(k), g(k), inv(k), ALU.mult, ALU.mult) \
                      .then_inc(n_ready.sem, 1)
                    if k:
                        lo_part(k - 1)
                lo_part(KT - 1)

            def pre_norm(L, q, n, col):
                ve.wait_ge(rstd_ready.sem, rstd_ready.at(L, n + 1))
                normed(L, q, lambda k: x[:, k], lambda k: pc[:, col + k:col + k + 1], lambda k: rstd[:])

            def gate_up(L, s):
                with ve.Fori(0, FT // 2) as f:
                    for j in range(2):
                        t = s * FT + j
                        ve.wait_ge(silu_ready.sem, silu_ready.at(L, t + 1) + f * 2)
                        ve.wait_ge(up_done.sem, up_done.at(L, t + 1) + f * 2)
                        ve.tensor_tensor(act_out[:, j], act_out[:, j], T(2 * j + 1), ALU.mult) \
                          .then_inc(h_ready.sem, 1)
                        ve.wait_ge(hh_ready.sem, hh_ready.at(L, t + 1) + f * 2)
                        at = bass.ds(f * 2 + j, 1)
                        ve.tensor_tensor(hl[:, at], act_out[:, j:j + 1], hh[:, at].bitcast(F32), ALU.subtract) \
                          .then_inc(hl_ready.sem, 1)

            def out_tiles(L, first, n, y):
                for d in range(KT):
                    ve.wait_ge(out_done.sem, out_done.at(L, first + d + 1))
                    ve.tensor_copy(y[:, d], T(d % 4)).then_inc(y_ready.sem, 1)
                    if d >= 2:
                        add_square(L, n, d - 1)
                add_square(L, n, KT - 1)

            def prepare(L):
                ve.wait_ge(par_loaded.sem, par_loaded.at(L, 2))
                lam = pc[:, LAM:LAM + 3]
                ve.tensor_scalar(dc[:, D_HALF1:D_HALF1 + 8], pc[:, G_F1POST:G_F1POST + 8], 0.5, None, ALU.mult)
                ve.tensor_scalar(dc[:, D_HALF2:D_HALF2 + 8], pc[:, G_F2POST:G_F2POST + 8], 0.5, None, ALU.mult)
                ve.scalar_tensor_tensor(sp[:, 0, 0:3], lam, -1.0, lam, ALU.mult, ALU.max).then_inc(lam_ready.sem, 1)
                e, s, u, q = (sp[:, i, 0:3] for i in range(1, 5))
                ve.wait_ge(lam_exp.sem, lam_exp.at(L, 1))
                link = steps.link
                link(ve.tensor_scalar(s, e, 2.0, None, ALU.add))
                link(ve.reciprocal(u, s))
                link(ve.tensor_tensor(s, e, u, ALU.mult))
                link(ve.tensor_tensor(u, s, s, ALU.mult))
                link(ve.tensor_scalar(q, u, 1.0 / 17, None, ALU.mult))
                for c in range(15, 1, -2):
                    link(ve.scalar_tensor_tensor(q, q, 1.0 / c, u, ALU.add, ALU.mult))
                link(ve.scalar_tensor_tensor(q, q, 1.0, s, ALU.add, ALU.mult))
                link(ve.tensor_scalar(e, lam, 0.0, 0.5, ALU.min, ALU.mult))
                link(ve.tensor_tensor(q, q, e, ALU.subtract))
                ve.tensor_scalar(dc[:, D_SPPOS:D_SPPOS + 3], q, 16.0, None, ALU.mult)
                ve.tensor_scalar(dc[:, D_SPNEG:D_SPNEG + 3], q, -16.0, None, ALU.mult).then_inc(dc_ready.sem, 1)
                ve.wait_ge(dc_ready.sem, dc_ready.at(L, 1))

            def mix_vector(L):
                link = steps.link
                ve.wait_ge(z_ready.sem, z_ready.at(L, NZ))
                link(ve.memset(va[:, :, :, HD:HD + 1], 1.0))
                ve.wait_ge(sb_loaded.sem, sb_loaded.at(L, 2))
                link(ve.tensor_copy(xs[:, :, :, 3:7], z[:, 0:3, SEQ:TOK].rearrange("p j (b t) -> p j b t", t=NT)))
                for tap in range(3, -1, -1):
                    s = 3 - tap
                    for j in range(3):
                        w = pc[:, CONV_W + 3 * tap + j:CONV_W + 3 * tap + j + 1]
                        out_p, in_p = xc[:, j, s:SEQ], z[:, j, 0:SEQ - s]
                        out_s = xc[:, j, SEQ:TOK].rearrange("p (b t) -> p b t", t=NT)
                        in_s = xs[:, j, :, tap:tap + NT]
                        if tap == 3:
                            b = pc[:, CONV_B + j:CONV_B + j + 1]
                            ve.tensor_scalar(out_p, in_p, w, b, ALU.mult, ALU.add)
                            ins = ve.tensor_scalar(out_s, in_s, w, b, ALU.mult, ALU.add)
                        else:
                            ve.scalar_tensor_tensor(out_p, in_p, w, out_p, ALU.mult, ALU.add)
                            ins = ve.scalar_tensor_tensor(out_s, in_s, w, out_s, ALU.mult, ALU.add)
                    if tap:
                        link(ins)
                ins.then_inc(xc_ready.sem, 1)
                ve.tensor_copy(sb_[:, S_CP:S_CS].rearrange("p (j t) -> p j t", j=3), z[:, 0:3, SEQ - 3:SEQ])
                ve.tensor_copy(sb_[:, S_CS:S_HP].rearrange("p (j b t) -> p j b t", j=3, b=NB), xs[:, :, :, 4:7])
                gb = z[:, ZGB:ZGB + 3, :]
                link(ve.tensor_tensor(ge[:], gb, gb, ALU.mult))
                link(ve.tensor_scalar(ge[:], ge[:], float(GELU_3), float(GELU_1), ALU.mult, ALU.add))
                ve.tensor_tensor(ge[:], ge[:], gb, ALU.mult).then_inc(ge_in.sem, 1)
                ve.wait_ge(rg_ready.sem, rg_ready.at(L, 6))
                ve.tensor_tensor(xc[:], xc[:], gt[:, :, 1, :], ALU.mult)
                ve.wait_ge(ab_ready.sem, ab_ready.at(L, 2))
                link(ve.tensor_tensor(gt[:, :, 0, :], av[:], av[:], ALU.mult))
                ve.scalar_tensor_tensor(gt[:, :, 0, :], gt[:, :, 0, :], 1.0, bv[:], ALU.add, ALU.mult) \
                  .then_inc(bb_ready.sem, 1)
                ve.wait_ge(bs_ready.sem, bs_ready.at(L, 1))
                link(ve.tensor_tensor(bv[:], bv[:], xc[:], ALU.mult))
                for j in range(3):
                    ve.tensor_tensor_scan(gt[:, j, 1, 0:SEQ], av[:, j, 0:SEQ], bv[:, j, 0:SEQ], 0.0, ALU.mult, ALU.add)
                a_s, b_s, h_s = (v.rearrange("p j (b t) -> p j b t", t=NT)
                                 for v in (av[:, :, SEQ:TOK], bv[:, :, SEQ:TOK], gt[:, :, 1, SEQ:TOK]))
                for t in range(NT):
                    before = h0[:] if t == 0 else h_s[:, :, :, t - 1]
                    link(ve.tensor_tensor(ht[:], a_s[:, :, :, t], before, ALU.mult))
                    link(ve.tensor_tensor(h_s[:, :, :, t], ht[:], b_s[:, :, :, t], ALU.add))
                ve.tensor_copy(sb_[:, S_HP:S_HS].rearrange("p (j o) -> p j o", o=1), gt[:, :, 1, SEQ - 1:SEQ])
                ve.tensor_copy(sb_[:, S_HS:NSB].rearrange("p (j b) -> p j b", j=3), h_s[:, :, :, NT - 1])
                ve.wait_ge(ge_out.sem, ge_out.at(L, 1))
                link(ve.tensor_tensor(gb, gb, ge[:], ALU.mult))
                ve.tensor_tensor(gb, gb, gt[:, :, 1, :], ALU.mult).then_inc(b_done.sem, 1)
                ve.wait_ge(b_done.sem, b_done.at(L, 1))

                ve.wait_ge(sb_stored.sem, sb_stored.at(L, 1))
                ig, fg = z[0:HC, ZGATE, :], z[32:32 + HC, ZGATE, :]
                R = lambda i: rows[:, i, :]
                link(ve.tensor_scalar(R(FB), fg, pc[32:32 + HC, B_F:B_F + 1], None, ALU.add))
                ve.scalar_tensor_tensor(R(DW), R(FB), -1.0, R(FB), ALU.mult, ALU.max).then_inc(fb_ready.sem, 1)
                link(ve.memset(mp[:, 0:1], 0.0))
                ve.wait_ge(fe_ready.sem, fe_ready.at(L, 1))
                link(ve.scalar_tensor_tensor(R(LF), R(FB), 0.0, R(DW), ALU.min, ALU.subtract))
                link(ve.tensor_tensor_scan(R(BR), con[0:HC, K_RST:K_RST + TOK], R(LF), 0.0, ALU.mult, ALU.add))
                ve.scalar_tensor_tensor(R(GR), ig, pc[0:HC, B_I:B_I + 1], R(BR), ALU.add, ALU.subtract) \
                  .then_inc(row_ready.sem, 1)
                ve.wait_ge(row_ready.sem, row_ready.at(L, 1))
                for t in range(4):
                    c = slice(t * P, (t + 1) * P)
                    e = slice((t + 1) * P - 1, (t + 1) * P)
                    link(ve.tensor_tensor_scan(rows[:, GG, c], rows[:, GR, c], rows[:, GR, c], mp[:, t:t + 1],
                                               ALU.max, ALU.max))
                    link(ve.tensor_tensor(mp[:, t + 1:t + 2], rows[:, BR, e], rows[:, GG, e], ALU.add))
                ve.wait_ge(sc_loaded.sem, sc_loaded.at(L, 2))
                g_s, gg_s, mt_s, dw_s = (rows[:, i, SEQ:TOK].rearrange("p (b t) -> p b t", t=NT)
                                         for i in (GR, GG, MT, DW))
                for t in range(NT):
                    before = m0[:] if t == 0 else gg_s[:, :, t - 1]
                    link(ve.tensor_tensor(gg_s[:, :, t], before, g_s[:, :, t], ALU.max))
                link(ve.tensor_tensor(R(MT), R(BR), R(GG), ALU.add))
                for t in range(4):
                    c = slice(t * P, (t + 1) * P)
                    ve.tensor_scalar(rows[:, DW, c], rows[:, GG, c], -1.0, mp[:, t:t + 1], ALU.mult, ALU.add)
                ve.tensor_copy(mo[:, 0:1], mp[:, 4:5])
                ve.tensor_copy(mo[:, 1:1 + NB], mt_s[:, :, NT - 1])
                m0b = m0[:].rearrange("p (b o) -> p b o", o=1).to_broadcast([HC, NB, NT])
                ve.tensor_tensor(dw_s, m0b, gg_s, ALU.subtract).then_inc(row_ready.sem, 1)
                ve.wait_ge(gc_done.sem, gc_done.at(L, 1))
                ve.tensor_copy(gc[:, 0:4, :], psum[:, 4, 0:16].rearrange("p (t h) -> p t h", h=HC))
                ve.tensor_copy(gc[0:32, 4, :], psum[0:32, 4, 16:20]).then_inc(gc_ready.sem, 1)
                ve.wait_ge(wb_ready.sem, wb_ready.at(L, 4))
                ve.tensor_tensor(qw[:], z[:, ZQC:ZQC + 2, :], wi[:], ALU.mult).then_inc(qw_ready.sem, 1)

                def weigh(t):
                    n = P if t < 4 else 32
                    ve.wait_ge(wm_ready.sem, wm_ready.at(L, t + 1))
                    ve.wait_ge(sc_done.sem, sc_done.at(L, t + 1))
                    if t:
                        ve.wait_ge(nd_done.sem, nd_done.at(L, t))
                    ve.scalar_tensor_tensor(
                        at_[0:n, :, 0:n], psum[0:n, 2 + t % 2, :].rearrange("p (h n) -> p h n", h=HC)[:, :, 0:n],
                        SCALE, wt[0:n, :, 0:n], ALU.mult, ALU.mult).then_inc(at_ready.sem, 1)
                    k = kc[0:n, t, :].rearrange("p (h d) -> p h d", h=HC)
                    if t < 4:
                        if t:
                            ve.wait_ge(cu_done.sem, cu_done.at(L, t))
                        ve.tensor_tensor(kw[:], k, wt[:, :, P - 1:P].to_broadcast([P, HC, HD]), ALU.mult) \
                          .then_inc(kw_ready.sem, 1)
                    else:
                        for b in range(NB):
                            e = NT * b + NT - 1
                            ins = ve.tensor_tensor(kwm[:, b], k, wt[0:32, :, e:e + 1].to_broadcast([32, HC, HD]),
                                                   ALU.mult)
                        ins.then_inc(kw_ready.sem, 1)

                def finish(t):
                    n = P if t < 4 else 32
                    c = slice(t * P, t * P + n)
                    ve.wait_ge(nd_done.sem, nd_done.at(L, t + 1))
                    num, den = (psum[:, 4 + t % 2, 256 * i:256 * i + 256].rearrange("p (c n) -> p c n", c=2)[:, :, 0:n]
                                for i in range(2))
                    link(ve.scalar_tensor_tensor(dn[:, :, 0:n], den, -1.0, em[:, :, c], ALU.mult, ALU.max))
                    link(ve.tensor_tensor(dn[:, :, 0:n], den, dn[:, :, 0:n], ALU.max))
                    link(ve.reciprocal(dn[:, :, 0:n], dn[:, :, 0:n]))
                    ve.tensor_tensor(hc[:, :, c], num, dn[:, :, 0:n], ALU.mult).then_inc(hc_ready.sem, 1)

                def update(t):
                    ve.wait_ge(cu_done.sem, cu_done.at(L, t + 1))
                    if t >= 1:
                        ve.wait_ge(cu_ready.sem, cu_ready.at(L, t))
                    for p in range(2):
                        r = slice(HD * p, HD * p + HD)
                        new = psum[r, 6 + t % 2, 0:260].rearrange("p (c n) -> p c n", c=2)[:, :, 65 * p:65 * p + 65]
                        if t == 0:
                            ins = ve.tensor_copy(cp[r], new)
                        else:
                            for c in range(2):
                                ins = ve.scalar_tensor_tensor(cp[r, c, :], cp[r, c, :],
                                                              wi[r, c, t * P + P - 1:t * P + P], new[:, c, :],
                                                              ALU.mult, ALU.add)
                    ins.then_inc(cu_ready.sem, 1)

                for t in range(4):
                    weigh(t)
                    finish(t)
                    update(t)
                weigh(4)
                finish(4)
                last = wi[:, :, SEQ:TOK].rearrange("p c (b t) -> p b c t", t=NT)[:, :, :, NT - 1:NT]
                for c in range(2):
                    ins = ve.tensor_tensor(cs[:, :, c, :], cs[:, :, c, :],
                                           last[:, :, c, :].to_broadcast([P, NB, HD + 1]), ALU.mult)
                link(ins)
                for b in range(NB):
                    ve.wait_ge(cu_done.sem, cu_done.at(L, 5 + b))
                    for p in range(2):
                        r = slice(HD * p, HD * p + HD)
                        new = psum[r, 6 + b % 2, 0:260].rearrange("p (c n) -> p c n", c=2)[:, :, 65 * p:65 * p + 65]
                        ins = ve.tensor_tensor(cs[r, b], cs[r, b], new, ALU.add)
                    ins.then_inc(cu_ready.sem, 1)
                ve.wait_ge(oc_ready.sem, oc_ready.at(L, 1))
                ve.wait_ge(hc_ready.sem, hc_ready.at(L, 5))
                ve.tensor_tensor(z[:, ZVC:ZVC + 2, :], hc[:], z[:, ZOC:ZOC + 2, :], ALU.mult).then_inc(c_done.sem, 1)

                def row_max(i, out, scores, mask):
                    s = stat[:, i % 2]
                    link(ve.tensor_tensor_reduce(out, scores, mask, 1.0, LOW, ALU.add, ALU.max, s[:, 0:1]))
                    ve.tensor_scalar(s[:, 1:2], s[:, 0:1], -SCALE, None, ALU.mult).then_inc(mx_ready.sem, 1)

                def row_sum(i, out, mask):
                    s = stat[:, i % 2]
                    ve.wait_ge(e_ready.sem, e_ready.at(L, i + 1))
                    link(ve.tensor_tensor_reduce(out, out, mask, 1.0, 0.0, ALU.mult, ALU.add, s[:, 2:3]))
                    link(ve.reciprocal(s[:, 3:4], s[:, 2:3]))
                    ve.tensor_scalar(out, out, s[:, 3:4], None, ALU.mult).then_inc(p_done.sem, 1)

                ve.wait_ge(z_stored.sem, z_stored.at(L, 2))
                ve.nop(nofuse=True)
                for i in range(24 + 3):
                    if i < 24:
                        n = (i % 4 + 1) * P
                        ve.wait_ge(s_done.sem, s_done.at(L, i + 1))
                        if i >= 2:
                            ve.wait_ge(pt_done.sem, pt_done.at(L, i - 1))
                        ve.nop(nofuse=True)
                        row_max(i, pp[:, i % 2, 0:n], psum[:, i % 4, 0:n], con[:, K_PADD + SEQ - n:K_PADD + SEQ])
                    if 1 <= i < 25:
                        n = ((i - 1) % 4 + 1) * P
                        row_sum(i - 1, pp[:, (i - 1) % 2, 0:n], con[:, K_PMUL + SEQ - n:K_PMUL + SEQ])
                    if i >= 3:
                        u = i - 3
                        r = slice(HD * (u // 4 % 2), HD * (u // 4 % 2) + HD)
                        ve.wait_ge(o_done.sem, o_done.at(L, u + 1))
                        ve.tensor_copy(z[r, ZV + u // 8, u % 4 * P:(u % 4 + 1) * P], psum[r, 6 + u % 2, 0:P]) \
                          .then_inc(o_ready.sem, 1)
                ve.wait_ge(qz_ready.sem, qz_ready.at(L, 1))
                for c in range(3):
                    for p in range(2):
                        r = slice(HD * p, HD * p + HD)
                        o = 8 * c + 4 * p
                        ins = ve.tensor_copy(qbd[r, :, c, o:o + NT],
                                             z[r, ZQ + c, SEQ:TOK].rearrange("p (b t) -> p b t", t=NT))
                ins.then_inc(q_ready.sem, 1)
                for g in range(2):
                    two = lambda v: v.rearrange("p (h n) -> p h n", h=2)
                    ve.wait_ge(kv_used.sem, kv_used.at(L, 8 * g + 4))
                    if g:
                        ve.wait_ge(pt_done.sem, pt_done.at(L, 26))
                    ve.nop(nofuse=True)
                    row_max(g, two(ps_[:, :]), psum[:, 2 * g:2 * g + 2, 0:KS // 2], two(con[:, K_SADD:K_SADD + KS]))
                    ve.wait_ge(mx_ready.sem, mx_ready.at(L, 25 + g))
                    s = stat[:, g]
                    ve.wait_ge(e_ready.sem, e_ready.at(L, 25 + g))
                    link(ve.tensor_tensor_reduce(ps_[:, :], ps_[:, :], con[:, K_SMUL:K_SMUL + KS], 1.0, 0.0,
                                                 ALU.mult, ALU.add, s[:, 2:3]))
                    link(ve.reciprocal(s[:, 3:4], s[:, 2:3]))
                    ve.tensor_scalar(ps_[:, :], ps_[:, :], s[:, 3:4], None, ALU.mult).then_inc(p_done.sem, 1)
                    ve.wait_ge(kv_used.sem, kv_used.at(L, 8 * g + 8))
                    for c in range(3):
                        for p in range(2):
                            r = slice(HD * p, HD * p + HD)
                            at = SEQ + KEYS_NEW * g
                            o = psum[r, 6 + g, 0:96].rearrange("p (j c q) -> p j c q", j=4, c=3)
                            ins = ve.tensor_copy(z[r, ZV + c, at:at + KEYS_NEW].rearrange("p (j t) -> p j t", t=NT),
                                                 o[:, :, c, 4 * p:4 * p + 4])
                    ins.then_inc(o_ready.sem, 1)

                def out_gain(k):
                    c = (G_A + k) if k < 3 else (G_B + k - 3) if k < 6 else (G_C + k - 6)
                    return pc[:, c:c + 1]
                ve.wait_ge(gr_ready.sem, gr_ready.at(L, 4))
                halves = lambda v: v.rearrange("p (h n) -> p h n", h=2)
                normed(L, N_OUT, lambda k: halves(z[:, OUT_TILES[k], :]), out_gain,
                       lambda k: gr[:, (0, 0, 0, 1, 1, 1, 2, 3)[k]])

            for i in range(1, KT):
                ve.wait_ge(sq_ready.sem, i + 1)
                if i > 1:
                    ve.wait_ge(sq_added.sem, i - 1)
                ve.tensor_tensor(acc[:], sq[:, 0] if i == 1 else acc[:], sq[:, i % 2], ALU.add) \
                  .then_inc(sq_added.sem, 1)
            ve.memset(sp[:], 0.0).then_inc(layer_done.sem, 1)
            for free in (h_ready, hl_ready, y_ready, ye_ready):
                ve.sem_inc(free.sem, free.ahead)
            with ve.Fori(0, DEPTH) as L:
                steps = Steps(ve, dve_steps, L)
                ve.wait_ge(layer_done.sem, L + 1)
                prepare(L)
                pre_norm(L, N_F1, 0, G_F1PRE)
                gate_up(L, 0)
                out_tiles(L, 0, 0, y_ff)
                add_norm(L, 0, 1, y_ff, dc[:, D_HALF1:D_HALF1 + 8])
                pre_norm(L, N_MIX, 2, G_MIXPRE)
                mix_vector(L)
                out_tiles(L, KT, 2, y_z)
                add_norm(L, 1, 3, y_z, pc[:, G_MIXPOST:G_MIXPOST + 8])
                pre_norm(L, N_F2, 4, G_F2PRE)
                gate_up(L, 1)
                out_tiles(L, 2 * KT, 4, y_ff)
                ve.wait_ge(p_ready.sem, p_ready.at(L, 1))
                ve.tensor_tensor(pl[:], pe_raw[:], ph[:].bitcast(F32), ALU.subtract).then_inc(p_ready.sem, 1)
                add_norm(L, 2, 5, y_ff, dc[:, D_HALF2:D_HALF2 + 8])
                for d in range(4):
                    ve.wait_ge(pj_done.sem, pj_done.at(L, d + 1))
                    ve.tensor_copy(y_z[:, d], T(d % 4)).then_inc(pj_ready.sem, 1)
                pre_norm(L, N_PLE, 6, G_PLEPRE)
                for d in range(4, KT):
                    ve.wait_ge(pj_done.sem, pj_done.at(L, d + 1))
                    ve.tensor_copy(y_z[:, d], T(d % 4)).then_inc(pj_ready.sem, 1)
                ve.wait_ge(pj_ready.sem, pj_ready.at(L, KT))
                for d in range(KT):
                    ve.wait_ge(pg_ready.sem, pg_ready.at(L, d + 1))
                    ve.tensor_tensor(y_z[:, d], y_z[:, d], act_out[:, d % 2], ALU.mult).then_inc(ye_ready.sem, 1)
                    if d >= 2:
                        add_square(L, 6, d - 1)
                add_square(L, 6, KT - 1)
                add_norm(L, 3, 7, y_z, pc[:, G_PLEPOST:G_PLEPOST + 8])
                ve.wait_ge(sq_added.sem, sq_added.at(L, 56))
                ve.sem_inc(layer_done.sem, 1)
                steps.end()

        @block.gpsimd
        def _(po):
            def lo_part(k, hi_value):
                po.wait_ge(hi.sem, hi_value)
                po.tensor_tensor(wl[:, k, :], raw[:, k, :], wh[:, k, :].bitcast(F32), ALU.subtract) \
                  .then_inc(lo.sem, 1)

            def lo_parts(L, first, count):
                with po.Fori(0, count // 2) as f:
                    for k in range(2):
                        lo_part(k, hi.at(L, first + k + 3) + f * 2)

            po.sem_inc(z_ready.sem, z_ready.ahead)
            po.sem_inc(pg_ready.sem, pg_ready.ahead)
            lo_part(0, 1)
            lo_part(1, 2)
            with po.Fori(0, DEPTH) as L:
                steps = Steps(po, pool_steps, L)
                lo_parts(L, CH_F1, CH_OUT - CH_F1)
                for t in range(5):
                    n = P if t < 4 else 32
                    w = wt[0:n, :, 0:n]
                    po.wait_ge(we_ready.sem, we_ready.at(L, t + 1))
                    po.nop(nofuse=True)
                    causal = po.affine_select(out=w, in_=w, pattern=[[0, HC], [1, n]], compare_op=ALU.is_ge,
                                              fill=0.0, base=0, channel_multiplier=-1)
                    if t < 4:
                        causal.then_inc(wm_ready.sem, 1)
                    else:
                        steps.link(causal, hold=True)
                        w = w.rearrange("p h (b t) -> p h b t", t=NT)
                        po.affine_select(out=w, in_=w, pattern=[[0, HC], [-NT, NB], [0, NT]],
                                         compare_op=ALU.is_ge, fill=0.0, base=0, channel_multiplier=1) \
                          .then_inc(wm_ready.sem, 1)
                po.wait_ge(cu_done.sem, cu_done.at(L, 4 + NB))
                po.nop(nofuse=True)
                po.memset(qbd[:], 0.0).then_inc(qz_ready.sem, 1)
                lo_parts(L, CH_OUT, CHUNKS - CH_OUT)
                steps.end()


def reached():
    old = [16 * g + t for t in range(4) for g in range(96)]
    return np.array(old + list(range(W_BUF - 512, W_BUF)))


def constants():
    c = np.zeros((P, NCONST), np.float32)
    c[:, K_ID:K_ID + P] = np.eye(P)
    c[:, K_ONE:K_ONE + P] = 1.0
    c[:64, K_BLK:K_BLK + 64] = 1.0
    c[64:, K_BLK + 64:K_BLK + 128] = 1.0

    def count(dist):
        return (((dist >= 0) & (dist <= 128)).astype(int)
                + ((dist >= 0) & (dist <= 512) & (dist % 4 == 0))
                + ((dist >= 0) & (dist <= 2048) & (dist % 16 == 0)))

    n = count(np.arange(P)[:, None] - (np.arange(SEQ)[None] - (SEQ - P)))
    c[:, K_PADD:K_PADD + SEQ] = np.where(n > 0, 0.0, NEG)
    c[:, K_PMUL:K_PMUL + SEQ] = n
    rows = reached()
    for j in range(4):
        for r in range(24):
            t = r % 4
            n = np.concatenate([count(W_BUF + t - rows), np.zeros(KEYS_NEW, int)])
            n[KEYS + 4 * j:KEYS + 4 * j + 4] = count(t - np.arange(4))
            c[32 * j + r, K_SADD:K_SADD + KS] = np.where(n > 0, 0.0, NEG)
            c[32 * j + r, K_SMUL:K_SMUL + KS] = n
        c[32 * j + 24:32 * j + 32, K_SMUL:K_SMUL + KS] = 1.0
    for h in range(HC):
        c[h, K_SELH + h * P:K_SELH + (h + 1) * P] = 1.0
        o = K_SEL2 + (h // 2) * P + (h % 2) * HD
        c[h, o:o + HD] = 1.0
    keep = np.ones(TOK, np.float32)
    keep[0:SEQ:P] = 0.0
    keep[SEQ::NT] = 0.0
    c[:, K_RST:K_RST + TOK] = keep
    return c


def lay_out(i):
    f32 = np.float32
    out = {}

    def feature_major(prompt, sample):
        a = np.concatenate([prompt.reshape(SEQ, -1), sample.reshape(NB * NT, -1)]).T
        return a.reshape(-1, P, 2, HALF).transpose(1, 0, 2, 3)

    out["x"] = feature_major(i["x_prompt"][0], i["x_sample"])
    out["pe"] = np.stack([feature_major(i["p_prompt"][l, 0], i["p_sample"][l]) for l in range(DEPTH)])

    w = np.zeros((DEPTH * CHUNKS + 2, P, 8, P), f32)
    splits = np.cumsum([0, 384, 384, 384, 384, 384, 256, 256, 256, 256, 4, 4])
    for l in range(DEPTH):
        o = l * CHUNKS
        for c0, g, u, d, c1 in ((CH_F1, "w_f1_gate", "w_f1_up", "w_f1_down", CH_D1),
                                (CH_F2, "w_f2_gate", "w_f2_up", "w_f2_down", CH_D2)):
            for n, name in enumerate((g, u)):
                w[o + c0 + n:o + c0 + C_UP:2] = i[name][l].reshape(KT, P, FT, P).transpose(2, 1, 0, 3)
            b = i[d][l].reshape(FT, P, KT, P).transpose(2, 1, 0, 3)
            at = 0
            for p, n in enumerate(DOWN_BLOCKS):
                w[o + c1 + p:o + c1 + C_DOWN:3, :, 0:n] = b[:, :, at:at + n]
                at += n
        s = i["w_in"][l]
        part = [s[:, splits[n]:splits[n + 1]] for n in range(11)]
        q, k, v, xb, gb, qc, kc, vc, oc, ic, fc = part
        gates = np.zeros((D, P), f32)
        gates[:, 0:4], gates[:, 32:36] = ic, fc
        s = np.concatenate([xb, gb, gates, qc, kc, vc, oc, q, k, v], axis=1)
        w[o + CH_IN:o + CH_IN + NZ] = s.reshape(KT, P, NZ, P).transpose(2, 1, 0, 3)
        for c0, name in ((CH_OUT, "w_out"), (CH_PG, "w_ple_gate")):
            w[o + c0:o + c0 + KT] = i[name][l].reshape(KT, P, KT, P).transpose(2, 1, 0, 3)
        b = i["w_ple_proj"][l].reshape(2, P, 2, 4, P).transpose(2, 1, 3, 0, 4)
        w[o + CH_PJ:o + CH_PJ + 2] = b.reshape(2, P, 8, P)
    out["weights"] = w.reshape(-1, P, 8 * P)

    par = np.zeros((DEPTH, P, NPAR), f32)

    def column(c, name):
        a = i[name].reshape(DEPTH, -1, P)
        par[:, :, c:c + a.shape[1]] = a.transpose(0, 2, 1)

    for c, name in ((G_F1PRE, "g_f1_pre"), (G_F1POST, "g_f1_post"), (G_MIXPRE, "g_mix_pre"),
                    (G_MIXPOST, "g_mix_post"), (G_F2PRE, "g_f2_pre"), (G_F2POST, "g_f2_post"),
                    (G_PLEPRE, "g_ple_pre"), (G_PLEPOST, "g_ple_post"), (CONV_W, "conv_w"), (CONV_B, "conv_b"),
                    (B_RA, "b_rg_a"), (B_RX, "b_rg_x"), (LAM, "lru_lambda"), (G_A, "g_out_a"),
                    (G_B, "g_out_b"), (G_C, "g_out_c")):
        column(c, name)
    par[:, 0:HC, B_I] = i["b_mlstm_i"]
    par[:, 32:32 + HC, B_F] = i["b_mlstm_f"]
    out["par"] = par
    rgw = np.zeros((DEPTH, P, 2, 3, P), f32)
    for n, name in enumerate(("w_rg_a", "w_rg_x")):
        for j in range(3):
            for p in range(2):
                rgw[:, 64 * p:64 * p + 64, n, j, 64 * p:64 * p + 64] = i[name][:, 2 * j + p]
    out["rgw"] = rgw
    out["consts"] = constants()

    rows = reached()
    k = i["cache_k"][:, :, rows].reshape(DEPTH, NB, KEYS, 3, P)
    out["kc"] = k.transpose(0, 1, 4, 3, 2).reshape(DEPTH, NB, P, 3 * KEYS)
    v = i["cache_v"][:, :, rows].reshape(DEPTH, NB, 7, P, 384)
    out["vc"] = v.transpose(0, 1, 3, 2, 4).reshape(DEPTH, NB, P, 7 * 384)
    out["sconv"] = i["state_conv"].reshape(DEPTH, NB, 3, 3, P).transpose(0, 4, 3, 1, 2)
    out["sh"] = i["state_h"].reshape(DEPTH, NB, 3, P).transpose(0, 3, 2, 1)
    c = np.concatenate([i["state_C"], i["state_n"][..., None]], axis=-1)
    out["sc"] = c.reshape(DEPTH, NB, 2, 2, HD, HD + 1).transpose(0, 3, 4, 1, 2, 5).reshape(DEPTH, P, NB, 2, HD + 1)
    out["sm"] = i["state_m"].transpose(0, 2, 1)
    return {n: np.ascontiguousarray(a) for n, a in out.items()}


OUTPUTS = dict(x=(P, KT, 2, HALF), k=(DEPTH, P, 3, TOK), v=(DEPTH, P, 3, TOK), sb=(DEPTH, P, NSB),
               cp=(DEPTH, P, 2, HD + 1), cs=(DEPTH, P, NB, 2, HD + 1), m=(DEPTH, HC, 1 + NB))


def kernel(**inputs):
    import concourse.bacc as bacc
    from concourse.bass_utils import run_bass_kernel_spmd

    arrays = lay_out({n: np.asarray(a) for n, a in inputs.items()})
    nc = bacc.Bacc("TRN2", target_bir_lowering=False, num_devices=1)
    ins = {n: nc.dram_tensor(f"in_{n}", list(a.shape), F32, kind="ExternalInput").ap() for n, a in arrays.items()}
    outs = {n: nc.dram_tensor(f"out_{n}", list(s), F32, kind="ExternalOutput").ap() for n, s in OUTPUTS.items()}
    build(nc, ins, outs)
    r = run_bass_kernel_spmd(nc, [{f"in_{n}": a for n, a in arrays.items()}], core_ids=[0])
    o = {n: np.asarray(r.results[0][f"out_{n}"]) for n in OUTPUTS}

    y = o["x"].transpose(1, 0, 2, 3).reshape(D, TOK).T
    y_prompt, y_sample = y[None, :SEQ], y[SEQ:].reshape(NB, NT, D)

    def rows_of(a):
        t = a.transpose(0, 3, 2, 1).reshape(DEPTH, TOK, HA, HD)
        return t[:, None, :SEQ], t[:, SEQ:].reshape(DEPTH, NB, NT, HA, HD)

    k_prompt, k_sample = rows_of(o["k"])
    v_prompt, v_sample = rows_of(o["v"])
    s = o["sb"]
    conv_prompt = s[:, :, S_CP:S_CS].reshape(DEPTH, P, 3, 3).transpose(0, 3, 2, 1).reshape(DEPTH, 1, 3, DB)
    conv_sample = s[:, :, S_CS:S_HP].reshape(DEPTH, P, 3, NB, 3).transpose(0, 3, 4, 2, 1).reshape(DEPTH, NB, 3, DB)
    h_prompt = s[:, :, S_HP:S_HS].transpose(0, 2, 1).reshape(DEPTH, 1, DB)
    h_sample = s[:, :, S_HS:NSB].reshape(DEPTH, P, 3, NB).transpose(0, 3, 2, 1).reshape(DEPTH, NB, DB)
    cp = o["cp"].reshape(DEPTH, 2, HD, 2, HD + 1).transpose(0, 3, 1, 2, 4).reshape(DEPTH, 1, HC, HD, HD + 1)
    cs = o["cs"].reshape(DEPTH, 2, HD, NB, 2, HD + 1).transpose(0, 3, 4, 1, 2, 5).reshape(DEPTH, NB, HC, HD, HD + 1)
    m_prompt = o["m"][:, :, 0][:, None]
    m_sample = o["m"][:, :, 1:].transpose(0, 2, 1)
    out = (y_prompt, y_sample, k_prompt, v_prompt, k_sample, v_sample, conv_prompt, conv_sample,
           h_prompt, h_sample, cp[..., :HD], cs[..., :HD], cp[..., HD], cs[..., HD], m_prompt, m_sample)
    return tuple(np.ascontiguousarray(a) for a in out)
```

```python
import numpy as np
from contextlib import ExitStack, contextmanager

import concourse.bass as bass
from concourse import mybir

F32 = mybir.dt.float32
F32R = mybir.dt.float32r
ALU = mybir.AluOpType
ACT = mybir.ActivationFunctionType
EXP_LN = "natural_log_exp_and_others"

P = 128
DEPTH, D, SEQ, NB, NT = 2, 1024, 512, 8, 4
TOK = SEQ + NB * NT
HALF = TOK // 2
DFF, HD, HA, HC, DB, DPLE = 2816, 64, 6, 4, 384, 256
KT = D // P
FT = DFF // P
W_BUF = 2048
KEYS = 512 + 384
KEYS_NEW = 16
KS = KEYS + KEYS_NEW
EPS = 1e-6
NEG = -1e30
LOW = -3.0e38
SCALE = HD ** -0.5

ZXB, ZGB, ZGATE, ZQC, ZKC, ZVC, ZOC, ZQ, ZK, ZV, NZ = 0, 3, 6, 7, 9, 11, 13, 15, 18, 21, 24
Z_C = 20
Z_B = 8
C_UP, C_DOWN, C_IN, C_OUT, C_PJ, C_PG = 2 * FT, 3 * KT, NZ, KT, 2, KT
CH_F1 = 0
CH_D1 = CH_F1 + C_UP
CH_IN = CH_D1 + C_DOWN
CH_OUT = CH_IN + C_IN
CH_F2 = CH_OUT + C_OUT
CH_D2 = CH_F2 + C_UP
CH_PJ = CH_D2 + C_DOWN
CH_PG = CH_PJ + C_PJ
CHUNKS = CH_PG + C_PG
DOWN_BLOCKS = (8, 7, 7)

(G_F1PRE, G_F1POST, G_MIXPRE, G_MIXPOST, G_F2PRE, G_F2POST, G_PLEPRE, G_PLEPOST) = range(0, 64, 8)
CONV_W, CONV_B, B_RA, B_RX, LAM, G_A, G_B, G_C, B_I, B_F, NPAR = 64, 76, 79, 82, 85, 88, 91, 94, 96, 97, 98
D_HALF1, D_HALF2, D_SPNEG, D_SPPOS, ND = 0, 8, 16, 19, 22
K_ID, K_ONE, K_BLK = 0, 128, 256
K_PADD, K_PMUL = 384, 896
K_SADD = 1408
K_SMUL = K_SADD + KS
K_SELH = K_SMUL + KS
K_SEL2 = K_SELH + 512
K_RST = K_SEL2 + 256
NCONST = K_RST + TOK
S_CP, S_CS, S_HP, S_HS, NSB = 0, 9, 81, 84, 108
GELU_1 = 2.0 * (2.0 / np.pi) ** 0.5
GELU_3 = GELU_1 * 0.044715

S_K, S_MAX, S_SUM, S_TURN, S_V, S_COPY, S_OUT = (((3, 4, 6, 7), (17, 18, 19, 20)), (8, 21), (9, 22), (10, 23),
                                                 ((11, 12, 13, 14), (24, 25, 26, 27)), (15, 28), (16, 29))
STEPS_A = 30

N_F1, N_MIX, N_OUT, N_F2, N_PLE = range(5)
OUT_TILES = (ZV, ZV + 1, ZV + 2, ZGB, ZGB + 1, ZGB + 2, ZVC, ZVC + 1)
LINKS_ACT, LINKS_DVE, LINKS_POOL, LINKS_PE = 13, 144, 1, 9


class Signal:

    def __init__(self, sem, per_layer, ahead=0, unit=1):
        self.sem, self.per, self.ahead, self.unit = sem, per_layer, ahead, unit

    def at(self, layer, n):
        return layer * (self.per * self.unit) + (n + self.ahead) * self.unit


class Steps:

    def __init__(self, eng, signal, layer):
        self.eng, self.s, self.layer = eng, signal, layer
        self.n = 0
        self.f, self.per_turn = 0, 0

    def link(self, ins, hold=False):
        ins.then_inc(self.s.sem, 1)
        self.n += 1
        self.eng.wait_ge(self.s.sem, self.s.at(self.layer, self.n + self.f * self.per_turn))
        if hold:
            self.eng.nop(nofuse=True)

    @contextmanager
    def loop(self, count, per_turn):
        with self.eng.Fori(0, count) as f:
            start = self.n
            self.f, self.per_turn = f, per_turn
            yield f
            assert self.n - start == per_turn, ("links in a turn", self.n - start)
            self.f, self.per_turn = 0, 0
            self.n = start + count * per_turn

    def end(self):
        assert self.n == self.s.per, (self.s.sem, "links in a layer", self.n, "stated", self.s.per)


def build(nc, I, O):
    x_in, weights, par, rgw, consts, pe_in = I["x"], I["weights"], I["par"], I["rgw"], I["consts"], I["pe"]
    ctx = ExitStack()
    with ctx:
        base = (nc.sbuf_base + 63) // 64 * 64
        here = [base]

        def place(name, shape, dt=F32, at=None):
            size = int(np.prod(shape[1:])) * 4
            offset = here[0] if at is None else at
            if at is None:
                here[0] += (size + 31) // 32 * 32
                assert here[0] <= nc.sbuf_usable_end, (name, here[0], nc.sbuf_usable_end)
            return nc.alloc_sbuf_tensor_at(name, shape, dt, offset=offset), offset, offset + (size + 31) // 32 * 32

        x, _, _ = place("x", [P, KT, 2, HALF])
        xh, a_xh, _ = place("xh", [P, KT, 2, HALF], F32R)
        xl, a_xl, e_xl = place("xl", [P, KT, 2, HALF], F32R)
        hh, a_h, _ = place("hh", [P, FT, 2, HALF], F32R)
        hl, _, e_h = place("hl", [P, FT, 2, HALF], F32R)
        raw, _, _ = place("raw", [P, 2, 8 * P])
        wh, _, _ = place("wh", [P, 2, 8 * P], F32R)
        wl, _, _ = place("wl", [P, 2, 8 * P], F32R)
        act_out, a_e, _ = place("act_out", [P, 2, 2, HALF])
        rstd, _, _ = place("rstd", [P, 2, HALF])
        acc, _, _ = place("acc", [P, 2, HALF])
        sq, a_sq, _ = place("sq", [P, 2, 2, HALF])
        tmp, a_tmp, _ = place("tmp", [P, 2, 2, HALF])
        con, _, _ = place("con", [P, NCONST])
        pc, _, _ = place("pc", [P, NPAR])
        dc, _, _ = place("dc", [P, ND])
        sp, _, _ = place("sp", [P, 5, 4])
        stat, _, _ = place("stat", [P, 3, 4])
        rg, _, _ = place("rg", [P, 2, 3, P])
        y_ff, _, _ = place("y_ff", [P, KT, 2, HALF], at=a_xl)
        z, _, a = place("z", [P, NZ, TOK], at=a_h)
        a_kv = a
        kv, _, e = place("kv", [P, 4, 7 * 384], at=a_kv)
        assert e <= e_h
        y_z, _, e = place("y_z", [P, KT, 2, HALF], at=a_h)
        pe_raw, _, e = place("pe_raw", [P, 2, 2, HALF], at=e)
        ph, _, e = place("ph", [P, 2, 2, HALF], F32R, at=e)
        pl, _, e = place("pl", [P, 2, 2, HALF], F32R, at=e)
        assert e <= e_h
        xc, _, e = place("xc", [P, 3, TOK], at=a_kv)
        gt, _, e = place("gt", [P, 3, 2, TOK], at=e)
        av, _, e = place("av", [P, 3, TOK], at=e)
        bv, _, e = place("bv", [P, 3, TOK], at=e)
        xs, _, e = place("xs", [P, 3, NB, 7], at=e)
        h0, _, e = place("h0", [P, 3, NB], at=e)
        sb_, _, e = place("sb", [P, NSB], at=e)
        ht, _, e = place("ht", [P, 3, NB], at=e)
        a_b2 = e
        rows, _, e = place("rows", [HC, 7, TOK], at=a_kv)
        LF, BR, GR, GG, MT, DW, FB = range(7)
        wi, _, e = place("wi", [P, 2, TOK], at=e)
        em, _, e = place("em", [P, 2, TOK], at=e)
        wt, _, e = place("wt", [P, HC, P], at=e)
        at_, _, e = place("at", [P, HC, P], at=e)
        gc, _, e = place("gc", [P, 5, HC], at=e)
        hc, _, e = place("hc", [P, 2, TOK], at=e)
        qw, _, e = place("qw", [P, 2, TOK], at=e)
        kw, _, e = place("kw", [P, HC, HD], at=e)
        dn, _, e = place("dn", [P, 2, P], at=e)
        mp, _, e = place("mp", [HC, 8], at=e)
        m0, _, e = place("m0", [HC, NB], at=e)
        assert e <= e_h, (e, e_h)
        vt, _, e = place("vt", [P, 4, 384], at=a_xh)
        vs, _, e = place("vs", [KEYS_NEW, 2, 384], at=e)
        kc, _, e = place("kc", [P, 5, HC * HD], at=e)
        va, _, e = place("va", [P, 5, HC, HD + 1], at=e)
        cs, _, e = place("cs", [P, NB, 2, HD + 1], at=e)
        cp, _, e = place("cp", [P, 2, HD + 1], at=e)
        a_w = e
        kwm, _, e = place("kwm", [32, NB, HC, HD], at=a_w)
        mo, _, e = place("mo", [HC, 1 + NB], at=e)
        assert e <= e_xl
        qbd, _, e = place("qbd", [P, NB, 3, 32], at=a_w)
        pts, _, e = place("pts", [P, 8, P], at=e)
        assert e <= e_xl, (e, e_xl)
        pp, _, _ = place("pp", [P, 2, SEQ], at=a_e)
        ptp, _, _ = place("ptp", [P, 2, 4, P], at=a_sq)
        ps_, _, _ = place("psm", [P, KS], at=a_tmp)
        ge, _, e = place("ge", [P, 3, TOK], at=a_sq)
        gr, _, _ = place("gr", [P, 4, 2, HALF], at=a_kv)

        psum = ctx.enter_context(nc.psum_tensor("psum", [P, 8, 512], F32))

        def T(i):
            return psum[:, 2 * i:2 * i + 2, 0:HALF]

        ident, ones, blk = con[:, K_ID:K_ID + P], con[:, K_ONE:K_ONE + P], con[:, K_BLK:K_BLK + P]

        def signal(name, per_layer, ahead=0, unit=1):
            return Signal(ctx.enter_context(nc.semaphore(name)), per_layer, ahead, unit)

        loaded = [signal(f"chunk_loaded_{s}", CHUNKS // 2, 0, 16) for s in range(2)]
        hi = signal("chunk_hi_ready", CHUNKS)
        lo = signal("chunk_lo_ready", CHUNKS)
        part_used = signal("down_part_used", 4 * KT)
        const_loaded = signal("const_loaded", 0, 0, 16)
        x_loaded = signal("x_loaded", 0, 0, 16)
        par_loaded = signal("par_loaded", 2, 0, 16)
        pe_loaded = signal("pe_loaded", 1, 0, 16)
        sb_loaded = signal("branch_state_loaded", 2, 0, 16)
        sc_loaded = signal("memory_state_loaded", 1, 0, 16)
        m0_loaded = signal("memory_max_loaded", 1, 0, 16)
        kv_loaded = [signal(f"kv_loaded_{s}", 4, 0, 16) for s in range(4)]
        z_stored = signal("kv_rows_stored", 2, 0, 16)
        sb_stored = signal("branch_state_stored", 1, 0, 16)
        sc_stored = signal("memory_state_stored", 3, 0, 16)
        x_stored = signal("x_stored", 0, 0, 16)
        layer_done = signal("layer_done", 1)
        sq_ready = signal("square_ready", 64, 8)
        sq_added = signal("square_added", 28)
        sq_used = signal("x_square_used", 32)
        yn_ready = signal("normed_y_ready", 32)
        stat_done = signal("y_mean_square_done", 4)
        rstd_ready = signal("rstd_ready", 8)
        n_ready = signal("normed_ready", 5 * KT)
        nh_ready = signal("normed_hi_ready", 5 * KT)
        nl_ready = signal("normed_lo_ready", 5 * KT)
        xn_ready = signal("x_ready", 32)
        gate_done = signal("gate_done", 2 * FT)
        up_done = signal("up_done", 2 * FT)
        silu_ready = signal("silu_ready", 2 * FT)
        h_ready = signal("h_ready", 2 * FT, 2)
        hh_ready = signal("h_hi_ready", 2 * FT)
        hl_ready = signal("h_lo_ready", 2 * FT, 2)
        out_done = signal("out_tile_done", 3 * KT)
        y_ready = signal("y_ready", 3 * KT, 4)
        z_done = signal("z_tile_done", NZ)
        z_ready = signal("z_ready", NZ, 2)
        p_ready = signal("pe_split_ready", 2)
        pj_done = signal("embedding_done", KT)
        pj_ready = signal("embedding_ready", KT)
        pg_done = signal("ple_gate_done", KT)
        pg_ready = signal("ple_gate_ready", KT, 2)
        ye_ready = signal("ple_y_ready", KT, 2)
        act_steps = signal("scalar_steps", LINKS_ACT)
        dve_steps = signal("vector_steps", LINKS_DVE)
        pe_steps = signal("tensor_steps", LINKS_PE)
        pool_steps = signal("pool_steps", LINKS_POOL)
        lam_ready = signal("lambda_abs_ready", 1)
        lam_exp = signal("lambda_exp_ready", 1)
        dc_ready = signal("derived_ready", 1)
        xc_ready = signal("conv_ready", 1)
        rg_done = signal("recurrent_gate_done", 6)
        rg_ready = signal("recurrent_gate_ready", 6)
        ab_ready = signal("decay_ready", 2)
        bb_ready = signal("one_minus_a2_ready", 1)
        bs_ready = signal("branch_input_scale_ready", 1)
        ge_in = signal("gelu_argument_ready", 1)
        ge_out = signal("gelu_gate_ready", 1)
        b_done = signal("branch_done", 1)
        tm_done = signal("transposed", 11)
        tm_ready = signal("token_major_ready", 11)
        fb_ready = signal("forget_abs_ready", 1)
        fe_ready = signal("forget_log_ready", 1)
        row_ready = signal("gate_rows_ready", 2)
        gc_done = signal("g_column_done", 1)
        gc_ready = signal("g_column_ready", 1)
        wb_done = signal("spread_done", 4)
        wb_ready = signal("spread_ready", 4)
        qw_ready = signal("q_weighted_ready", 1)
        gb_done = signal("g_spread_done", 5)
        we_ready = signal("weight_exp_ready", 5)
        wm_ready = signal("weight_masked_ready", 5)
        sc_done = signal("qk_done", 5)
        at_ready = signal("a_ready", 5)
        kw_ready = signal("k_weighted_ready", 5)
        nd_done = signal("num_den_done", 5)
        hc_ready = signal("memory_read_ready", 5)
        cu_done = signal("memory_update_done", 4 + NB)
        cu_ready = signal("memory_ready", 4 + NB)
        oc_ready = signal("output_gate_ready", 1)
        c_done = signal("memory_group_done", 1)
        s_done = signal("scores_done", 24)
        mx_ready = signal("row_max_ready", 24)
        e_ready = signal("exp_ready", 24)
        p_done = signal("probs_ready", 24)
        pt_done = signal("probs_transposed", 24)
        pt_ready = signal("probs_token_major", 24)
        o_done = signal("attention_out_done", 24)
        o_ready = signal("attention_out_ready", 24)
        smx_ready = signal("sample_row_max_ready", 2)
        se_ready = signal("sample_exp_ready", 2)
        sp_done = signal("sample_probs_ready", 2)
        spt_done = signal("sample_probs_transposed", 4)
        spt_ready = signal("sample_probs_token_major", 4)
        so_copied = signal("sample_out_copied", 2)
        so_turned = signal("sample_out_turned", 2)
        so_ready = signal("sample_out_ready", 2)
        q_ready = signal("q_blocks_ready", 1)
        qz_ready = signal("q_blocks_zeroed", 1)
        kv_used = signal("kv_used", 16)
        gs_ready = signal("group_square_ready", 8)
        gst_done = signal("group_mean_done", 4)
        gr_ready = signal("group_rstd_ready", 4)

        block = ctx.enter_context(nc.Block())

        @block.sync
        def _(sy):
            sy.dma_start(con[:, :], consts).then_inc(const_loaded.sem, 16)
            for k in range(2):
                sy.dma_start(raw[:, k, :], weights[k]).then_inc(loaded[k].sem, 16)
            sy.dma_start(x[:], x_in).then_inc(x_loaded.sem, 16)
            with sy.Fori(0, DEPTH) as L:
                def chunks(first, count):
                    with sy.Fori(0, count // 2) as f:
                        for k in range(2):
                            sy.wait_ge(lo.sem, lo.at(L, first + k + 1) + f * 2)
                            sy.dma_start(raw[:, k, :], weights[L * CHUNKS + f * 2 + (first + k + 2)]) \
                              .then_inc(loaded[k].sem, 16)

                sy.wait_ge(layer_done.sem, L + 1)
                sy.dma_start(pc[:, :], par[L]).then_inc(par_loaded.sem, 16)
                sy.dma_start(rg[:], rgw[L]).then_inc(par_loaded.sem, 16)
                chunks(CH_F1, CH_IN + 2 - CH_F1)
                sy.wait_ge(out_done.sem, out_done.at(L, KT))
                sy.dma_start(xs[:, :, :, 0:3], I["sconv"][L]).then_inc(sb_loaded.sem, 16)
                sy.dma_start(h0[:], I["sh"][L]).then_inc(sb_loaded.sem, 16)
                chunks(CH_IN + 2, Z_C)
                sy.wait_ge(b_done.sem, b_done.at(L, 1))
                sy.dma_start(O["sb"][L], sb_[:, :]).then_inc(sb_stored.sem, 16)
                sy.dma_start(m0[:], I["sm"][L]).then_inc(m0_loaded.sem, 16)
                chunks(CH_IN + 2 + Z_C, CH_OUT - CH_IN - Z_C)
                sy.wait_ge(z_done.sem, z_done.at(L, NZ))
                sy.dma_start(cs[:], I["sc"][L]).then_inc(sc_loaded.sem, 16)
                sy.wait_ge(z_ready.sem, z_ready.at(L, NZ))
                sy.dma_start(O["k"][L], z[:, ZK:ZK + 3, :]).then_inc(z_stored.sem, 16)
                sy.dma_start(O["v"][L], z[:, ZV:ZV + 3, :]).then_inc(z_stored.sem, 16)
                sy.wait_ge(c_done.sem, c_done.at(L, 1))
                for n in range(16):
                    g, what, j = n // 8, n % 8 // 4, n % 4
                    if n >= 4:
                        sy.wait_ge(kv_used.sem, kv_used.at(L, n - 3))
                    sy.dma_start(kv[:, n % 4, :], (I["kc"] if what == 0 else I["vc"])[L, 4 * g + j]) \
                      .then_inc(kv_loaded[n % 4].sem, 16)
                    if n == 3:
                        sy.dma_start(O["cp"][L], cp[:]).then_inc(sc_stored.sem, 16)
                        sy.dma_start(O["cs"][L], cs[:]).then_inc(sc_stored.sem, 16)
                        sy.dma_start(O["m"][L], mo[:]).then_inc(sc_stored.sem, 16)
                chunks(CH_OUT + 2, CH_D2 - CH_OUT - 2)
                chunks(CH_D2, C_DOWN)
                sy.wait_ge(out_done.sem, out_done.at(L, 3 * KT))
                sy.dma_start(pe_raw[:], pe_in[L]).then_inc(pe_loaded.sem, 16)
                chunks(CH_PJ, C_PJ + C_PG)
            sy.wait_ge(layer_done.sem, DEPTH + 1)
            sy.dma_start(O["x"], x[:]).then_inc(x_stored.sem, 16)
            sy.wait_ge(x_stored.sem, 16)
            sy.wait_ge(z_stored.sem, 16 * 2 * DEPTH)
            sy.wait_ge(sb_stored.sem, 16 * DEPTH)
            sy.wait_ge(sc_stored.sem, 16 * 3 * DEPTH)
            sy.wait_ge(loaded[0].sem, 16 * (CHUNKS // 2 * DEPTH + 1))
            sy.wait_ge(loaded[1].sem, 16 * (CHUNKS // 2 * DEPTH + 1))

        @block.tensor
        def _(pe):
            def mean_square(L, n):
                pe.wait_ge(sq_added.sem, sq_added.at(L, 7 * n + 7))
                for h in range(2):
                    ins = pe.matmul(T(0)[:, h, :], ones, acc[:, h, :], start=True, stop=True)
                ins.then_inc(stat_done.sem, 1)

            def x_mean_square(sq_base):
                for k in range(KT):
                    pe.wait_ge(sq_ready.sem, sq_base + (k + 1))
                    for h in range(2):
                        ins = pe.matmul(T(0)[:, h, :], ones, sq[:, k % 2, h, :], start=(k == 0), stop=(k == KT - 1))
                    ins.then_inc(sq_used.sem, 1)

            def block3(out, slot, b, rh, rl, first, last):
                w_h, w_l = wh[:, slot, b * P:(b + 1) * P], wl[:, slot, b * P:(b + 1) * P]
                for n, (w, r) in enumerate(((w_h, rh), (w_h, rl), (w_l, rh))):
                    for h in range(2):
                        ins = pe.matmul(out[:, h, :], w, r[:, h, :], start=first and n == 0,
                                        stop=last and n == 2)
                return ins

            def gate_up(L, s):
                pre = (N_F1, N_F2)[s]
                c0 = (CH_F1, CH_F2)[s]
                with pe.Fori(0, FT // 2) as f:
                    for j in range(2):
                        pe.wait_ge(h_ready.sem, h_ready.at(L, s * FT + j - 1) + f * 2)
                        pe.wait_ge(lo.sem, lo.at(L, c0 + 2 * j + 1) + f * 4)
                        for k in range(KT):
                            pe.wait_ge(nl_ready.sem, nl_ready.at(L, pre * KT + k + 1))
                            ins = block3(T(2 * j), 0, k, xh[:, k], xl[:, k], k == 0, k == KT - 1)
                        ins.then_inc(gate_done.sem, 1)
                        pe.wait_ge(lo.sem, lo.at(L, c0 + 2 * j + 2) + f * 4)
                        for k in range(KT):
                            ins = block3(T(2 * j + 1), 1, k, xh[:, k], xl[:, k], k == 0, k == KT - 1)
                        ins.then_inc(up_done.sem, 1)

            def out_tiles(L, first, c0, ff):
                per = 3 if ff else 1
                with pe.Fori(0, 2) as f:
                    for j in range(4):
                        pe.wait_ge(y_ready.sem, y_ready.at(L, first + j - 3) + f * 4)
                        k = 0
                        for p in range(per):
                            c = j * per + p
                            pe.wait_ge(lo.sem, lo.at(L, c0 + c + 1) + f * (4 * per))
                            for b in range(DOWN_BLOCKS[p] if ff else KT):
                                rh, rl = (hh, hl) if ff else (xh, xl)
                                last = b == (DOWN_BLOCKS[p] if ff else KT) - 1
                                ins = block3(T(j), c % 2, b, rh[:, k], rl[:, k], k == 0,
                                             p == per - 1 and last)
                                k += 1
                            if p < per - 1:
                                ins.then_inc(part_used.sem, 1)
                        ins.then_inc(out_done.sem, 1)

            def recurrent_gates(L, j):
                if j == 0:
                    pe.wait_ge(par_loaded.sem, par_loaded.at(L, 2))
                    pe.wait_ge(xc_ready.sem, xc_ready.at(L, 1))
                for i in range(2):
                    if j:
                        pe.wait_ge(rg_ready.sem, rg_ready.at(L, 2 * j - 1 + i))
                    for h in range(2):
                        ins = pe.matmul(T(2 + i)[:, h, :], rg[:, i, j, :], xc[:, j, h * HALF:(h + 1) * HALF],
                                        start=True, stop=True)
                    ins.then_inc(rg_done.sem, 1)

            def mix_tensor(pe, L):
                pe.wait_ge(rg_ready.sem, rg_ready.at(L, 6))
                unit = 0
                for t in range(4):
                    cols = slice(t * P, (t + 1) * P)
                    for tiles in ((ZV, ZV + 1, ZV + 2), (ZKC, ZKC + 1, ZVC, ZVC + 1)):
                        if unit >= 4:
                            pe.wait_ge(tm_ready.sem, tm_ready.at(L, unit - 3))
                        for n, k in enumerate(tiles):
                            ins = pe.transpose(psum[:, 4 + unit % 4, n * P:(n + 1) * P], z[:, k, cols], ident)
                        ins.then_inc(tm_done.sem, 1)
                        unit += 1
                for g in range(2):
                    pe.wait_ge(tm_ready.sem, tm_ready.at(L, unit - 3))
                    for n in range(3):
                        ins = pe.transpose(psum[0:KEYS_NEW, 4 + unit % 4, n * P:(n + 1) * P],
                                           z[:, ZV + n, SEQ + KEYS_NEW * g:SEQ + KEYS_NEW * (g + 1)], ident)
                    ins.then_inc(tm_done.sem, 1)
                    unit += 1
                pe.wait_ge(tm_ready.sem, tm_ready.at(L, unit - 3))
                for n, k in enumerate((ZKC, ZKC + 1, ZVC, ZVC + 1)):
                    ins = pe.transpose(psum[0:32, 4 + unit % 4, n * P:(n + 1) * P], z[:, k, SEQ:TOK], ident)
                ins.then_inc(tm_done.sem, 1)
                pe.wait_ge(tm_ready.sem, tm_ready.at(L, 11))

                pe.wait_ge(row_ready.sem, row_ready.at(L, 1))
                pe.nop(nofuse=True)
                for t in range(5):
                    n = P if t < 4 else 32
                    ins = pe.transpose(psum[0:n, 4, t * HC:(t + 1) * HC], rows[:, GR, t * P:t * P + n],
                                       ident[0:HC, 0:HC])
                ins.then_inc(gc_done.sem, 1)
                pe.wait_ge(gc_ready.sem, gc_ready.at(L, 1))
                pe.wait_ge(row_ready.sem, row_ready.at(L, 2))
                for w, row in enumerate((DW, MT)):
                    for c in range(2):
                        t = T(2 * w + c)
                        for h in range(2):
                            ins = pe.matmul(t[:, h, :], con[0:HC, K_SEL2 + c * P:K_SEL2 + (c + 1) * P],
                                            rows[:, row, h * HALF:(h + 1) * HALF], start=True, stop=True)
                        ins.then_inc(wb_done.sem, 1)
                pe.wait_ge(wb_ready.sem, wb_ready.at(L, 4))

                def spread_g(t):
                    n = P if t < 4 else 32
                    if t >= 2:
                        pe.wait_ge(we_ready.sem, we_ready.at(L, t - 1))
                    for h in range(HC):
                        ins = pe.matmul(psum[:, t % 2, h * P:h * P + n],
                                        con[0:HC, K_SELH + h * P:K_SELH + (h + 1) * P],
                                        rows[:, GG, t * P:t * P + n], start=True, stop=True)
                    ins.then_inc(gb_done.sem, 1)

                def qk(t):
                    n = P if t < 4 else 32
                    if t >= 2:
                        pe.wait_ge(at_ready.sem, at_ready.at(L, t - 1))
                        pe.nop(nofuse=True)
                    for h in (0, 2, 1, 3):
                        r = slice(HD * (h % 2), HD * (h % 2) + HD)
                        if h == 1:
                            steps.link(ins, hold=True)
                        ins = pe.matmul(psum[0:n, 2 + t % 2, h * P:h * P + n], z[r, ZKC + h // 2, t * P:t * P + n],
                                        z[r, ZQC + h // 2, t * P:t * P + n], start=True, stop=True)
                    ins.then_inc(sc_done.sem, 1)

                def read(t):
                    n = P if t < 4 else 32
                    if t >= 2:
                        pe.wait_ge(hc_ready.sem, hc_ready.at(L, t - 1))
                    pe.wait_ge(at_ready.sem, at_ready.at(L, t + 1))
                    if t == 1:
                        pe.wait_ge(qw_ready.sem, qw_ready.at(L, 1))
                    if 1 <= t < 4:
                        pe.wait_ge(cu_ready.sem, cu_ready.at(L, t))
                    if t == 4:
                        pe.wait_ge(sc_loaded.sem, sc_loaded.at(L, 1))
                    for p in range(2):
                        if p and t:
                            steps.link(ins)
                        for c in range(2):
                            h, r = 2 * c + p, slice(HD * p, HD * p + HD)
                            for den in range(2):
                                o = psum[r, 4 + t % 2, den * 256 + c * P:den * 256 + c * P + n]
                                w = va[0:n, t, h, 0:HD] if not den else con[0:n, K_ONE:K_ONE + HD]
                                ins = pe.matmul(o, w, at_[0:n, h, 0:n], start=True, stop=(t == 0))
                                if 1 <= t < 4:
                                    w = cp[r, c, 0:HD] if not den else cp[r, c, HD:HD + 1].to_broadcast([HD, HD])
                                    ins = pe.matmul(o, w, qw[r, c, t * P:t * P + n], start=False, stop=True)
                                if t == 4:
                                    for b in range(NB):
                                        w = (cs[r, b, c, 0:HD] if not den
                                             else cs[r, b, c, HD:HD + 1].to_broadcast([HD, HD]))
                                        k = den * 256 + c * P + NT * b
                                        ins = pe.matmul(psum[r, 4 + t % 2, k:k + NT], w,
                                                        qw[r, c, SEQ + NT * b:SEQ + NT * b + NT],
                                                        start=False, stop=(b == NB - 1))
                    ins.then_inc(nd_done.sem, 1)

                def update(t):
                    pe.wait_ge(kw_ready.sem, kw_ready.at(L, t + 1))
                    if t < 4:
                        if t >= 2:
                            pe.wait_ge(cu_ready.sem, cu_ready.at(L, t - 1))
                        for c in range(2):
                            ins = pe.matmul(psum[:, 6 + t % 2, c * 130:(c + 1) * 130], kw[:, 2 * c:2 * c + 2, :],
                                            va[:, t, 2 * c:2 * c + 2, :], start=True, stop=True)
                        ins.then_inc(cu_done.sem, 1)
                    else:
                        for b in range(NB):
                            pe.wait_ge(cu_ready.sem, cu_ready.at(L, 4 + b - 1))
                            for c in range(2):
                                ins = pe.matmul(psum[:, 6 + b % 2, c * 130:(c + 1) * 130],
                                                kwm[:, b, 2 * c:2 * c + 2, :], va[0:32, 4, 2 * c:2 * c + 2, :],
                                                start=True, stop=True)
                            ins.then_inc(cu_done.sem, 1)

                spread_g(0)
                qk(0)
                for t in range(5):
                    if t < 4:
                        spread_g(t + 1)
                        qk(t + 1)
                    read(t)
                    update(t)
                pe.wait_ge(hc_ready.sem, hc_ready.at(L, 5))
                pe.wait_ge(cu_ready.sem, cu_ready.at(L, 4 + NB))

                def scores(u):
                    h, qb = u // 4, u % 4
                    r, n = slice(HD * (h % 2), HD * (h % 2) + HD), (qb + 1) * P
                    if u >= 2:
                        pe.wait_ge(mx_ready.sem, mx_ready.at(L, u - 1))
                    pe.matmul(psum[:, u % 2, 0:n], z[r, ZQ + h // 2, qb * P:(qb + 1) * P],
                              z[r, ZK + h // 2, 0:n], start=True, stop=True).then_inc(s_done.sem, 1)

                def turn(u):
                    pe.wait_ge(p_done.sem, p_done.at(L, u + 1))
                    if u >= 2:
                        pe.wait_ge(pt_ready.sem, pt_ready.at(L, u - 1))
                    for kb in range(u % 4 + 1):
                        ins = pe.transpose(psum[:, 4 + u % 2, kb * P:(kb + 1) * P],
                                           pp[:, u % 2, kb * P:(kb + 1) * P], ident)
                    ins.then_inc(pt_done.sem, 1)

                def values(u):
                    h, qb = u // 4, u % 4
                    r = slice(HD * (h % 2), HD * (h % 2) + HD)
                    pe.wait_ge(pt_ready.sem, pt_ready.at(L, u + 1))
                    if u >= 2:
                        pe.wait_ge(o_ready.sem, o_ready.at(L, u - 1))
                    for kb in range(qb + 1):
                        ins = pe.matmul(psum[r, 6 + u % 2, 0:P], vt[:, kb, h * HD:(h + 1) * HD],
                                        ptp[:, u % 2, kb, :], start=(kb == 0), stop=(kb == qb))
                    ins.then_inc(o_done.sem, 1)

                cut = KS // 2

                def sample_scores(g, j):
                    if g and j == 0:
                        pe.wait_ge(so_ready.sem, so_ready.at(L, 1))
                    b = 4 * g + j
                    pe.wait_ge(kv_loaded[j].sem, kv_loaded[j].at(L, 2 * g + 1))
                    rr = slice(32 * j, 32 * j + 32)
                    k_t = kv[:, j, 0:3 * KEYS].rearrange("p (c n) -> p c n", c=3)
                    for o0, n, src in ((0, cut, k_t[:, :, 0:cut]), (512, KEYS - cut, k_t[:, :, cut:KEYS]),
                                       (512 + KEYS - cut, KEYS_NEW,
                                        z[:, ZK:ZK + 3, SEQ + KEYS_NEW * g:SEQ + KEYS_NEW * (g + 1)])):
                        for c in range(3):
                            ins = pe.matmul(psum[rr, 2 + o0 // 512, o0 % 512:o0 % 512 + n], qbd[:, b, c, :],
                                            src[:, c, :], start=(c == 0), stop=(c == 2))
                    ins.then_inc(kv_used.sem, 1)

                def sample_turn(g):
                    pe.wait_ge(sp_done.sem, sp_done.at(L, g + 1))
                    for q in range(2):
                        for kb in range(4 * q, 4 * q + 4):
                            n = P if kb < 7 else KEYS_NEW
                            ins = pe.transpose(psum[0:n, 2 + q, kb % 4 * P:(kb % 4 + 1) * P],
                                               ps_[:, kb * P:kb * P + n], ident)
                        ins.then_inc(spt_done.sem, 1)

                def sample_values(g, j):
                    if j == 0:
                        pe.wait_ge(spt_ready.sem, spt_ready.at(L, 2 * g + 2))
                    pe.wait_ge(kv_loaded[j].sem, kv_loaded[j].at(L, 2 * g + 2))
                    rr = slice(32 * j, 32 * j + 32)
                    for kb in range(7):
                        pe.matmul(psum[rr, 2, 0:384], pts[:, kb, rr], kv[:, j, kb * 384:(kb + 1) * 384],
                                  start=(kb == 0), stop=False)
                    pe.matmul(psum[rr, 2, 0:384], pts[0:KEYS_NEW, 7, rr], vs[:, g, :],
                              start=False, stop=True).then_inc(kv_used.sem, 1)

                def sample_out(g):
                    pe.wait_ge(so_copied.sem, so_copied.at(L, g + 1))
                    for c in range(3):
                        ins = pe.transpose(psum[:, 3, c * P:(c + 1) * P], ps_[:, c * P:(c + 1) * P], ident)
                    ins.then_inc(so_turned.sem, 1)

                for i in range(STEPS_A):
                    if i < 24:
                        scores(i)
                    if 2 <= i < 26:
                        turn(i - 2)
                    if 3 <= i < 27:
                        values(i - 3)
                    if i == 0:
                        pe.wait_ge(q_ready.sem, q_ready.at(L, 1))
                    for g in range(2):
                        if i in S_K[g]:
                            sample_scores(g, S_K[g].index(i))
                        if i == S_TURN[g]:
                            sample_turn(g)
                        if i in S_V[g]:
                            sample_values(g, S_V[g].index(i))
                        if i == S_OUT[g]:
                            sample_out(g)
                pe.wait_ge(o_ready.sem, o_ready.at(L, 24))
                pe.wait_ge(so_ready.sem, so_ready.at(L, 2))

                first = 0
                for n, tiles in enumerate((3, 3, 1, 1)):
                    for k in range(tiles):
                        pe.wait_ge(gs_ready.sem, gs_ready.at(L, first + 1))
                        for h in range(2):
                            ins = pe.matmul(T(n)[:, h, :], ones if n < 2 else blk, y_ff[:, first, h, :],
                                            start=(k == 0), stop=(k == tiles - 1))
                        first += 1
                    ins.then_inc(gst_done.sem, 1)

            def x_sum(L, m):
                x_mean_square(sq_ready.at(L, 16 * m + 8))

            pe.wait_ge(const_loaded.sem, 16)
            x_mean_square(0)
            with pe.Fori(0, DEPTH) as L:
                steps = Steps(pe, pe_steps, L)
                gate_up(L, 0)
                pe.wait_ge(hl_ready.sem, hl_ready.at(L, FT))
                pe.nop(nofuse=True)
                out_tiles(L, 0, CH_D1, True)
                mean_square(L, 0)
                x_sum(L, 0)
                def z_tile(first, j, f=None):
                    more = 0 if f is None else f * 4
                    pe.wait_ge(z_ready.sem, z_ready.at(L, first + j - 1) + more)
                    pe.wait_ge(lo.sem, lo.at(L, CH_IN + first + j + 1) + more)
                    for k in range(KT):
                        pe.wait_ge(nl_ready.sem, nl_ready.at(L, N_MIX * KT + k + 1))
                        ins = block3(T(j % 2), j % 2, k, xh[:, k], xl[:, k], k == 0, k == KT - 1)
                    ins.then_inc(z_done.sem, 1)
                with pe.Fori(0, Z_B // 4) as f:
                    for j in range(4):
                        z_tile(0, j, f)
                for j in range(4):
                    z_tile(Z_B, j)
                    if j < 3:
                        recurrent_gates(L, j)
                with pe.Fori(0, (NZ - Z_B) // 4 - 1) as f:
                    for j in range(4):
                        z_tile(Z_B + 4, j, f)
                pe.wait_ge(z_ready.sem, z_ready.at(L, NZ))
                mix_tensor(pe, L)
                pe.wait_ge(nl_ready.sem, nl_ready.at(L, (N_OUT + 1) * KT))
                pe.nop(nofuse=True)
                out_tiles(L, KT, CH_OUT, False)
                mean_square(L, 1)
                x_sum(L, 1)
                gate_up(L, 1)
                pe.wait_ge(hl_ready.sem, hl_ready.at(L, 2 * FT))
                pe.nop(nofuse=True)
                out_tiles(L, 2 * KT, CH_D2, True)
                mean_square(L, 2)
                pe.wait_ge(p_ready.sem, p_ready.at(L, 2))
                pe.wait_ge(rstd_ready.sem, rstd_ready.at(L, 6))
                for d in range(KT):
                    if d % 4 == 0:
                        pe.wait_ge(lo.sem, lo.at(L, CH_PJ + d // 4 + 1))
                    if d == 4:
                        pe.wait_ge(pj_ready.sem, pj_ready.at(L, 4))
                        x_sum(L, 2)
                        pe.wait_ge(rstd_ready.sem, rstd_ready.at(L, 7))
                    for k in range(2):
                        ins = block3(T(d % 4), d // 4, d % 4 * 2 + k, ph[:, k], pl[:, k], k == 0, k == 1)
                    ins.then_inc(pj_done.sem, 1)
                pe.wait_ge(pj_ready.sem, pj_ready.at(L, KT))
                pe.nop(nofuse=True)
                with pe.Fori(0, KT // 2) as f:
                    for j in range(2):
                        pe.wait_ge(pg_ready.sem, pg_ready.at(L, j - 1) + f * 2)
                        pe.wait_ge(lo.sem, lo.at(L, CH_PG + j + 1) + f * 2)
                        for k in range(KT):
                            pe.wait_ge(nl_ready.sem, nl_ready.at(L, N_PLE * KT + k + 1))
                            ins = block3(T(j), j, k, xh[:, k], xl[:, k], k == 0, k == KT - 1)
                        ins.then_inc(pg_done.sem, 1)
                pe.wait_ge(pg_ready.sem, pg_ready.at(L, KT))
                mean_square(L, 3)
                x_sum(L, 3)
                steps.end()

        @block.scalar
        def _(act):
            def split(slot, loads):
                act.wait_ge(loaded[slot].sem, loads)
                act.copy(wh[:, slot, :], raw[:, slot, :]).then_inc(hi.sem, 1)

            def loads(L, c, f=None, per=0):
                n = loaded[0].at(L, (c + 2) // 2 + 1)
                return n if f is None else n + f * (8 * per)

            def square(L, m, k, src):
                if k >= 2:
                    act.wait_ge(sq_added.sem, sq_added.at(L, 7 * m + max(k - 2, 1)))
                act.activation(sq[:, k % 2], src, ACT.Square).then_inc(sq_ready.sem, 1)

            def inverse_rms(L, n):
                if n % 2:
                    act.wait_ge(stat_done.sem, stat_done.at(L, n // 2 + 1))
                else:
                    act.wait_ge(sq_used.sem, sq_used.at(L, n // 2 * KT + KT))
                steps.link(act.activation(rstd[:], T(0), ACT.Ln, bias=EPS, scale=1.0 / D))
                act.activation(rstd[:], rstd[:], ACT.Exp, scale=-0.5).then_inc(rstd_ready.sem, 1)

            def x_squares(L, m):
                for k in range(KT):
                    act.wait_ge(xn_ready.sem, xn_ready.at(L, m * KT + k + 1))
                    if k >= 2:
                        act.wait_ge(sq_used.sem, sq_used.at(L, (m + 1) * KT + k - 1))
                    act.activation(sq[:, k % 2], x[:, k], ACT.Square).then_inc(sq_ready.sem, 1)

            def normed_hi(L, q):
                for k in range(KT):
                    act.wait_ge(n_ready.sem, n_ready.at(L, q * KT + k + 1))
                    act.copy(xh[:, k], tmp[:, k % 2]).then_inc(nh_ready.sem, 1)

            def gate_up(L, s):
                c0 = (CH_F1, CH_F2)[s]
                act.preload_act_table(ACT.Silu)
                with act.Fori(0, FT // 2) as f:
                    for j in range(2):
                        t = s * FT + j
                        act.wait_ge(gate_done.sem, gate_done.at(L, t + 1) + f * 2)
                        act.wait_ge(hl_ready.sem, hl_ready.at(L, t - 1) + f * 2)
                        act.activation(act_out[:, j], T(2 * j), ACT.Silu).then_inc(silu_ready.sem, 1)
                        split(0, loads(L, c0 + 2 * j, f, 4))
                        act.wait_ge(up_done.sem, up_done.at(L, t + 1) + f * 2)
                        split(1, loads(L, c0 + 2 * j + 1, f, 4))
                        act.wait_ge(h_ready.sem, h_ready.at(L, t + 1) + f * 2)
                        act.copy(hh[:, bass.ds(f * 2 + j, 1)], act_out[:, j:j + 1]).then_inc(hh_ready.sem, 1)

            def out_tiles(L, first, c0, s, n, y):
                per = 1 if s is None else 3
                for d in range(KT):
                    for p in range(per):
                        c = d * per + p
                        if p < per - 1:
                            act.wait_ge(part_used.sem, part_used.at(L, 2 * (s * KT + d) + p + 1))
                        else:
                            act.wait_ge(out_done.sem, out_done.at(L, first + d + 1))
                        split(c % 2, loads(L, c0 + c))
                    act.wait_ge(y_ready.sem, y_ready.at(L, first + d + 1))
                    square(L, n, d, y[:, d])

            def recurrent_sigmoids(L, j):
                for i in range(2):
                    act.wait_ge(rg_done.sem, rg_done.at(L, 2 * j + i + 1))
                    b_ = pc[:, (B_RA, B_RX)[i] + j:(B_RA, B_RX)[i] + j + 1]
                    act.activation(gt[:, j, i, :].rearrange("p (h n) -> p h n", h=2), T(2 + i),
                                   ACT.Sigmoid, bias=b_).then_inc(rg_ready.sem, 1)

            def recurrent_scalar(L, step):
                if step == 0:
                    act.wait_ge(ge_in.sem, ge_in.at(L, 1))
                    act.activation(ge[:], ge[:], ACT.Sigmoid).then_inc(ge_out.sem, 1)
                elif step == 1:
                    act.wait_ge(dc_ready.sem, dc_ready.at(L, 1))
                    act.wait_ge(rg_ready.sem, rg_ready.at(L, 6))
                    for j in range(3):
                        ins = act.activation(bv[:, j, :], gt[:, j, 0, :], ACT.Tanh,
                                             scale=dc[:, D_SPPOS + j:D_SPPOS + j + 1])
                    ins.then_inc(ab_ready.sem, 1)
                elif step == 2:
                    for j in range(3):
                        ins = act.activation(av[:, j, :], gt[:, j, 0, :], ACT.Exp,
                                             scale=dc[:, D_SPNEG + j:D_SPNEG + j + 1])
                    ins.then_inc(ab_ready.sem, 1)
                elif step == 4:
                    act.wait_ge(bb_ready.sem, bb_ready.at(L, 1))
                    act.activation(bv[:], gt[:, :, 0, :], ACT.Sqrt).then_inc(bs_ready.sem, 1)

            def mix_scalar(L):
                act.wait_ge(z_done.sem, z_done.at(L, NZ))
                for u in range(11):
                    b = 4 + u % 4
                    act.wait_ge(tm_done.sem, tm_done.at(L, u + 1))
                    if u < 8 and u % 2 == 0:
                        act.copy(vt[:, u // 2, :], psum[:, b, 0:384]).then_inc(tm_ready.sem, 1)
                    elif u in (8, 9):
                        act.copy(vs[:, u - 8, :], psum[0:KEYS_NEW, b, 0:384]).then_inc(tm_ready.sem, 1)
                    else:
                        t, r = (u // 2, slice(0, P)) if u < 8 else (4, slice(0, 32))
                        act.mul(kc[r, t, :], psum[r, b, 0:256], SCALE)
                        act.copy(va[r, t, :, 0:HD],
                                 psum[r, b, 256:512].rearrange("p (h d) -> p h d", h=HC)).then_inc(tm_ready.sem, 1)
                for w, dst in enumerate((wi, em)):
                    for c in range(2):
                        act.wait_ge(wb_done.sem, wb_done.at(L, 2 * w + c + 1))
                        act.activation(dst[:, c, :].rearrange("p (h n) -> p h n", h=2), T(2 * w + c), ACT.Exp,
                                       scale=(1.0, -1.0)[w]).then_inc(wb_ready.sem, 1)
                act.wait_ge(gc_ready.sem, gc_ready.at(L, 1))
                for t in range(5):
                    n = P if t < 4 else 32
                    act.wait_ge(gb_done.sem, gb_done.at(L, t + 1))
                    if t:
                        act.wait_ge(kw_ready.sem, kw_ready.at(L, t))
                    for h in range(HC):
                        ins = act.activation(wt[0:n, h, 0:n], psum[0:n, t % 2, h * P:h * P + n], ACT.Exp,
                                             scale=-1.0, bias=gc[0:n, t, h:h + 1])
                    ins.then_inc(we_ready.sem, 1)

                for i in range(STEPS_A):
                    if i < 24:
                        act.wait_ge(mx_ready.sem, mx_ready.at(L, i + 1))
                        n = (i % 4 + 1) * P
                        act.activation(pp[:, i % 2, 0:n], pp[:, i % 2, 0:n], ACT.Exp, scale=SCALE,
                                       bias=stat[:, i % 2, 1:2]).then_inc(e_ready.sem, 1)
                    if 2 <= i < 26:
                        u = i - 2
                        n = (u % 4 + 1)
                        act.wait_ge(pt_done.sem, pt_done.at(L, u + 1))
                        if u >= 2:
                            act.wait_ge(o_done.sem, o_done.at(L, u - 1))
                        act.copy(ptp[:, u % 2, 0:n, :],
                                 psum[:, 4 + u % 2, 0:n * P].rearrange("p (k n) -> p k n", n=P))                            .then_inc(pt_ready.sem, 1)
                    for g in range(2):
                        if i == S_MAX[g]:
                            act.wait_ge(smx_ready.sem, smx_ready.at(L, g + 1))
                            act.activation(ps_[:, :], ps_[:, :], ACT.Exp, scale=SCALE,
                                           bias=stat[:, 2, 1:2]).then_inc(se_ready.sem, 1)
                        if i == S_TURN[g]:
                            for q in range(2):
                                act.wait_ge(spt_done.sem, spt_done.at(L, 2 * g + q + 1))
                                if g:
                                    act.wait_ge(kv_used.sem, kv_used.at(L, 8))
                                src = psum[:, 2 + q, :].rearrange("p (k n) -> p k n", n=P)
                                if q == 0:
                                    act.copy(pts[:, 0:4, :], src).then_inc(spt_ready.sem, 1)
                                else:
                                    act.copy(pts[:, 4:7, :], src[:, 0:3, :])
                                    act.copy(pts[0:KEYS_NEW, 7, :], src[0:KEYS_NEW, 3, :]).then_inc(spt_ready.sem, 1)

                act.wait_ge(o_ready.sem, o_ready.at(L, 24))
                act.wait_ge(so_ready.sem, so_ready.at(L, 2))
                act.wait_ge(sc_stored.sem, sc_stored.at(L, 3))
                for k, src in enumerate(OUT_TILES):
                    act.activation(y_ff[:, k].rearrange("p h n -> p (h n)"), z[:, src, :], ACT.Square) \
                       .then_inc(gs_ready.sem, 1)
                for n in range(4):
                    act.wait_ge(gst_done.sem, gst_done.at(L, n + 1))
                    steps.link(act.activation(gr[:, n], T(n), ACT.Ln, bias=EPS,
                                              scale=1.0 / (DB if n < 2 else HD)))
                    act.activation(gr[:, n], gr[:, n], ACT.Exp, scale=-0.5).then_inc(gr_ready.sem, 1)

            split(0, 16)
            split(1, 16)
            act.wait_ge(x_loaded.sem, 16)
            for k in range(KT):
                if k >= 2:
                    act.wait_ge(sq_used.sem, k - 1)
                act.activation(sq[:, k % 2], x[:, k], ACT.Square).then_inc(sq_ready.sem, 1)
            act.preload_act_table_set(EXP_LN)
            with act.Fori(0, DEPTH) as L:
                steps = Steps(act, act_steps, L)
                act.wait_ge(lam_ready.sem, lam_ready.at(L, 1))
                act.activation(sp[:, 1, :], sp[:, 0, :], ACT.Exp, scale=-1.0).then_inc(lam_exp.sem, 1)
                inverse_rms(L, 0)
                normed_hi(L, N_F1)
                gate_up(L, 0)
                out_tiles(L, 0, CH_D1, 0, 0, y_ff)
                act.preload_act_table_set(EXP_LN)
                inverse_rms(L, 1)
                x_squares(L, 0)
                inverse_rms(L, 2)
                normed_hi(L, N_MIX)
                def z_tile(first, j, f=None):
                    act.wait_ge(z_done.sem, z_done.at(L, first + j + 1) + (0 if f is None else f * 4))
                    split(j % 2, loads(L, CH_IN + first + j, f, 4))
                    dst = z[:, first + j, :] if f is None else z[:, bass.ds(f * 4 + (first + j), 1), :]
                    dst = (dst.rearrange("p (h n) -> p h n", h=2) if f is None
                           else dst.rearrange("p k (h n) -> p (k h) n", h=2))
                    act.copy(dst, T(j % 2)).then_inc(z_ready.sem, 1)
                with act.Fori(0, Z_B // 4) as f:
                    for j in range(4):
                        z_tile(0, j, f)
                for j in range(4):
                    z_tile(Z_B, j)
                    if j < 3:
                        recurrent_sigmoids(L, j)
                    else:
                        recurrent_scalar(L, 0)
                for j in range(4, 9):
                    z_tile(Z_B, j)
                    recurrent_scalar(L, j - 3)
                act.wait_ge(z_ready.sem, z_ready.at(L, ZOC + 2))
                act.activation(z[:, ZOC:ZOC + 2, :], z[:, ZOC:ZOC + 2, :], ACT.Sigmoid).then_inc(oc_ready.sem, 1)
                for j in range(9, NZ - Z_B):
                    z_tile(Z_B, j)
                    if Z_B + j == Z_C + 2:
                        act.preload_act_table_set(EXP_LN)
                        act.wait_ge(fb_ready.sem, fb_ready.at(L, 1))
                        steps.link(act.activation(rows[:, DW, :], rows[:, DW, :], ACT.Exp, scale=-1.0))
                        act.activation(rows[:, DW, :], rows[:, DW, :], ACT.Ln, bias=1.0).then_inc(fe_ready.sem, 1)
                mix_scalar(L)
                normed_hi(L, N_OUT)
                out_tiles(L, KT, CH_OUT, None, 1, y_z)
                inverse_rms(L, 3)
                x_squares(L, 1)
                inverse_rms(L, 4)
                normed_hi(L, N_F2)
                gate_up(L, 1)
                out_tiles(L, 2 * KT, CH_D2, 1, 2, y_ff)
                act.wait_ge(pe_loaded.sem, pe_loaded.at(L, 1))
                act.copy(ph[:], pe_raw[:]).then_inc(p_ready.sem, 1)
                act.preload_act_table_set(EXP_LN)
                inverse_rms(L, 5)
                act.wait_ge(pj_done.sem, pj_done.at(L, 4))
                split(0, loads(L, CH_PJ))
                x_squares(L, 2)
                inverse_rms(L, 6)
                normed_hi(L, N_PLE)
                act.wait_ge(pj_done.sem, pj_done.at(L, KT))
                split(1, loads(L, CH_PJ + 1))
                act.preload_act_table(ACT.Sigmoid)
                for d in range(KT):
                    act.wait_ge(pg_done.sem, pg_done.at(L, d + 1))
                    split(d % 2, loads(L, CH_PG + d))
                    act.wait_ge(ye_ready.sem, ye_ready.at(L, d - 1))
                    act.activation(act_out[:, d % 2], T(d % 2), ACT.Sigmoid).then_inc(pg_ready.sem, 1)
                    act.wait_ge(ye_ready.sem, ye_ready.at(L, d + 1))
                    square(L, 3, d, y_z[:, d])
                act.preload_act_table_set(EXP_LN)
                inverse_rms(L, 7)
                x_squares(L, 3)
                steps.end()

        @block.vector
        def _(ve):
            def add_square(L, m, i):
                ve.wait_ge(sq_ready.sem, sq_ready.at(L, 16 * m + i + 1))
                if i == 1:
                    a = sq[:, 0]
                else:
                    ve.wait_ge(sq_added.sem, sq_added.at(L, 7 * m + i - 1))
                    a = acc[:]
                ve.tensor_tensor(acc[:], a, sq[:, i % 2], ALU.add).then_inc(sq_added.sem, 1)

            def add_norm(L, m, n, y, g):
                ve.wait_ge(rstd_ready.sem, rstd_ready.at(L, n + 1))
                for k in range(KT + 1):
                    if k < KT:
                        ve.scalar_tensor_tensor(y[:, k], y[:, k], g[:, k:k + 1], rstd[:], ALU.mult, ALU.mult) \
                          .then_inc(yn_ready.sem, 1)
                    if k:
                        ve.wait_ge(yn_ready.sem, yn_ready.at(L, m * KT + k))
                        ve.tensor_tensor(x[:, k - 1], x[:, k - 1], y[:, k - 1], ALU.add).then_inc(xn_ready.sem, 1)

            def normed(L, q, src, g, inv):
                def lo_part(k):
                    ve.wait_ge(nh_ready.sem, nh_ready.at(L, q * KT + k + 1))
                    ve.tensor_tensor(xl[:, k], tmp[:, k % 2], xh[:, k].bitcast(F32), ALU.subtract) \
                      .then_inc(nl_ready.sem, 1)
                for k in range(KT):
                    if k >= 2:
                        ve.wait_ge(nl_ready.sem, nl_ready.at(L, q * KT + k - 1))
                    ve.scalar_tensor_tensor(tmp[:, k % 2], src(k), g(k), inv(k), ALU.mult, ALU.mult) \
                      .then_inc(n_ready.sem, 1)
                    if k:
                        lo_part(k - 1)
                lo_part(KT - 1)

            def pre_norm(L, q, n, col):
                ve.wait_ge(rstd_ready.sem, rstd_ready.at(L, n + 1))
                normed(L, q, lambda k: x[:, k], lambda k: pc[:, col + k:col + k + 1], lambda k: rstd[:])

            def gate_up(L, s):
                with ve.Fori(0, FT // 2) as f:
                    for j in range(2):
                        t = s * FT + j
                        ve.wait_ge(silu_ready.sem, silu_ready.at(L, t + 1) + f * 2)
                        ve.wait_ge(up_done.sem, up_done.at(L, t + 1) + f * 2)
                        ve.tensor_tensor(act_out[:, j], act_out[:, j], T(2 * j + 1), ALU.mult) \
                          .then_inc(h_ready.sem, 1)
                        ve.wait_ge(hh_ready.sem, hh_ready.at(L, t + 1) + f * 2)
                        at = bass.ds(f * 2 + j, 1)
                        ve.tensor_tensor(hl[:, at], act_out[:, j:j + 1], hh[:, at].bitcast(F32), ALU.subtract) \
                          .then_inc(hl_ready.sem, 1)

            def out_tiles(L, first, n, y):
                for d in range(KT):
                    ve.wait_ge(out_done.sem, out_done.at(L, first + d + 1))
                    ve.tensor_copy(y[:, d], T(d % 4)).then_inc(y_ready.sem, 1)
                    if d >= 2:
                        add_square(L, n, d - 1)
                add_square(L, n, KT - 1)

            def prepare(L):
                ve.wait_ge(par_loaded.sem, par_loaded.at(L, 2))
                lam = pc[:, LAM:LAM + 3]
                ve.tensor_scalar(dc[:, D_HALF1:D_HALF1 + 8], pc[:, G_F1POST:G_F1POST + 8], 0.5, None, ALU.mult)
                ve.tensor_scalar(dc[:, D_HALF2:D_HALF2 + 8], pc[:, G_F2POST:G_F2POST + 8], 0.5, None, ALU.mult)
                ve.scalar_tensor_tensor(sp[:, 0, 0:3], lam, -1.0, lam, ALU.mult, ALU.max).then_inc(lam_ready.sem, 1)
                e, s, u, q = (sp[:, i, 0:3] for i in range(1, 5))
                ve.wait_ge(lam_exp.sem, lam_exp.at(L, 1))
                link = steps.link
                link(ve.tensor_scalar(s, e, 2.0, None, ALU.add))
                link(ve.reciprocal(u, s))
                link(ve.tensor_tensor(s, e, u, ALU.mult))
                link(ve.tensor_tensor(u, s, s, ALU.mult))
                link(ve.tensor_scalar(q, u, 1.0 / 17, None, ALU.mult))
                for c in range(15, 1, -2):
                    link(ve.scalar_tensor_tensor(q, q, 1.0 / c, u, ALU.add, ALU.mult))
                link(ve.scalar_tensor_tensor(q, q, 1.0, s, ALU.add, ALU.mult))
                link(ve.tensor_scalar(e, lam, 0.0, 0.5, ALU.min, ALU.mult))
                link(ve.tensor_tensor(q, q, e, ALU.subtract))
                ve.tensor_scalar(dc[:, D_SPPOS:D_SPPOS + 3], q, 16.0, None, ALU.mult)
                ve.tensor_scalar(dc[:, D_SPNEG:D_SPNEG + 3], q, -16.0, None, ALU.mult).then_inc(dc_ready.sem, 1)
                ve.wait_ge(dc_ready.sem, dc_ready.at(L, 1))

            def mix_vector(L):
                link = steps.link
                ve.wait_ge(z_ready.sem, z_ready.at(L, 3))
                ve.wait_ge(sb_loaded.sem, sb_loaded.at(L, 2))
                link(ve.tensor_copy(xs[:, :, :, 3:7], z[:, 0:3, SEQ:TOK].rearrange("p j (b t) -> p j b t", t=NT)))
                for tap in range(3, -1, -1):
                    s = 3 - tap
                    for j in range(3):
                        w = pc[:, CONV_W + 3 * tap + j:CONV_W + 3 * tap + j + 1]
                        out_p, in_p = xc[:, j, s:SEQ], z[:, j, 0:SEQ - s]
                        out_s = xc[:, j, SEQ:TOK].rearrange("p (b t) -> p b t", t=NT)
                        in_s = xs[:, j, :, tap:tap + NT]
                        if tap == 3:
                            b = pc[:, CONV_B + j:CONV_B + j + 1]
                            ve.tensor_scalar(out_p, in_p, w, b, ALU.mult, ALU.add)
                            ins = ve.tensor_scalar(out_s, in_s, w, b, ALU.mult, ALU.add)
                        else:
                            ve.scalar_tensor_tensor(out_p, in_p, w, out_p, ALU.mult, ALU.add)
                            ins = ve.scalar_tensor_tensor(out_s, in_s, w, out_s, ALU.mult, ALU.add)
                    if tap:
                        link(ins)
                ins.then_inc(xc_ready.sem, 1)
                ve.tensor_copy(sb_[:, S_CP:S_CS].rearrange("p (j t) -> p j t", j=3), z[:, 0:3, SEQ - 3:SEQ])
                ve.tensor_copy(sb_[:, S_CS:S_HP].rearrange("p (j b t) -> p j b t", j=3, b=NB), xs[:, :, :, 4:7])
                ve.wait_ge(z_ready.sem, z_ready.at(L, 6))
                gb = z[:, ZGB:ZGB + 3, :]
                link(ve.tensor_tensor(ge[:], gb, gb, ALU.mult))
                link(ve.tensor_scalar(ge[:], ge[:], float(GELU_3), float(GELU_1), ALU.mult, ALU.add))
                ve.tensor_tensor(ge[:], ge[:], gb, ALU.mult).then_inc(ge_in.sem, 1)
                ve.wait_ge(rg_ready.sem, rg_ready.at(L, 6))
                ve.tensor_tensor(xc[:], xc[:], gt[:, :, 1, :], ALU.mult)
                ve.wait_ge(ab_ready.sem, ab_ready.at(L, 2))
                link(ve.tensor_tensor(gt[:, :, 0, :], av[:], av[:], ALU.mult))
                ve.scalar_tensor_tensor(gt[:, :, 0, :], gt[:, :, 0, :], 1.0, bv[:], ALU.add, ALU.mult) \
                  .then_inc(bb_ready.sem, 1)
                ve.wait_ge(bs_ready.sem, bs_ready.at(L, 1))
                link(ve.tensor_tensor(bv[:], bv[:], xc[:], ALU.mult))
                for j in range(3):
                    ve.tensor_tensor_scan(gt[:, j, 1, 0:SEQ], av[:, j, 0:SEQ], bv[:, j, 0:SEQ], 0.0, ALU.mult, ALU.add)
                a_s, b_s, h_s = (v.rearrange("p j (b t) -> p j b t", t=NT)
                                 for v in (av[:, :, SEQ:TOK], bv[:, :, SEQ:TOK], gt[:, :, 1, SEQ:TOK]))
                for t in range(NT):
                    before = h0[:] if t == 0 else h_s[:, :, :, t - 1]
                    link(ve.tensor_tensor(ht[:], a_s[:, :, :, t], before, ALU.mult))
                    link(ve.tensor_tensor(h_s[:, :, :, t], ht[:], b_s[:, :, :, t], ALU.add))
                ve.tensor_copy(sb_[:, S_HP:S_HS].rearrange("p (j o) -> p j o", o=1), gt[:, :, 1, SEQ - 1:SEQ])
                ve.tensor_copy(sb_[:, S_HS:NSB].rearrange("p (j b) -> p j b", j=3), h_s[:, :, :, NT - 1])
                ve.wait_ge(ge_out.sem, ge_out.at(L, 1))
                link(ve.tensor_tensor(gb, gb, ge[:], ALU.mult))
                ve.tensor_tensor(gb, gb, gt[:, :, 1, :], ALU.mult).then_inc(b_done.sem, 1)
                ve.wait_ge(b_done.sem, b_done.at(L, 1))

                ve.wait_ge(z_ready.sem, z_ready.at(L, ZGATE + 1))
                ve.wait_ge(sb_stored.sem, sb_stored.at(L, 1))
                ig, fg = z[0:HC, ZGATE, :], z[32:32 + HC, ZGATE, :]
                R = lambda i: rows[:, i, :]
                link(ve.tensor_scalar(R(FB), fg, pc[32:32 + HC, B_F:B_F + 1], None, ALU.add))
                ve.scalar_tensor_tensor(R(DW), R(FB), -1.0, R(FB), ALU.mult, ALU.max).then_inc(fb_ready.sem, 1)
                link(ve.memset(mp[:, 0:1], 0.0))
                ve.wait_ge(fe_ready.sem, fe_ready.at(L, 1))
                link(ve.scalar_tensor_tensor(R(LF), R(FB), 0.0, R(DW), ALU.min, ALU.subtract))
                link(ve.tensor_tensor_scan(R(BR), con[0:HC, K_RST:K_RST + TOK], R(LF), 0.0, ALU.mult, ALU.add))
                ve.scalar_tensor_tensor(R(GR), ig, pc[0:HC, B_I:B_I + 1], R(BR), ALU.add, ALU.subtract) \
                  .then_inc(row_ready.sem, 1)
                ve.wait_ge(row_ready.sem, row_ready.at(L, 1))
                for t in range(4):
                    c = slice(t * P, (t + 1) * P)
                    e = slice((t + 1) * P - 1, (t + 1) * P)
                    link(ve.tensor_tensor_scan(rows[:, GG, c], rows[:, GR, c], rows[:, GR, c], mp[:, t:t + 1],
                                               ALU.max, ALU.max))
                    link(ve.tensor_tensor(mp[:, t + 1:t + 2], rows[:, BR, e], rows[:, GG, e], ALU.add))
                ve.wait_ge(m0_loaded.sem, m0_loaded.at(L, 1))
                g_s, gg_s, mt_s, dw_s = (rows[:, i, SEQ:TOK].rearrange("p (b t) -> p b t", t=NT)
                                         for i in (GR, GG, MT, DW))
                for t in range(NT):
                    before = m0[:] if t == 0 else gg_s[:, :, t - 1]
                    link(ve.tensor_tensor(gg_s[:, :, t], before, g_s[:, :, t], ALU.max))
                link(ve.tensor_tensor(R(MT), R(BR), R(GG), ALU.add))
                for t in range(4):
                    c = slice(t * P, (t + 1) * P)
                    ve.tensor_scalar(rows[:, DW, c], rows[:, GG, c], -1.0, mp[:, t:t + 1], ALU.mult, ALU.add)
                ve.wait_ge(z_done.sem, z_done.at(L, NZ))
                link(ve.memset(va[:, :, :, HD:HD + 1], 1.0))
                ve.tensor_copy(mo[:, 0:1], mp[:, 4:5])
                ve.tensor_copy(mo[:, 1:1 + NB], mt_s[:, :, NT - 1])
                m0b = m0[:].rearrange("p (b o) -> p b o", o=1).to_broadcast([HC, NB, NT])
                ve.tensor_tensor(dw_s, m0b, gg_s, ALU.subtract).then_inc(row_ready.sem, 1)
                ve.wait_ge(gc_done.sem, gc_done.at(L, 1))
                ve.tensor_copy(gc[:, 0:4, :], psum[:, 4, 0:16].rearrange("p (t h) -> p t h", h=HC))
                ve.tensor_copy(gc[0:32, 4, :], psum[0:32, 4, 16:20]).then_inc(gc_ready.sem, 1)
                ve.wait_ge(wb_ready.sem, wb_ready.at(L, 4))
                ve.tensor_tensor(qw[:], z[:, ZQC:ZQC + 2, :], wi[:], ALU.mult).then_inc(qw_ready.sem, 1)

                def weigh(t):
                    n = P if t < 4 else 32
                    ve.wait_ge(wm_ready.sem, wm_ready.at(L, t + 1))
                    ve.wait_ge(sc_done.sem, sc_done.at(L, t + 1))
                    if t:
                        ve.wait_ge(nd_done.sem, nd_done.at(L, t))
                    ve.scalar_tensor_tensor(
                        at_[0:n, :, 0:n], psum[0:n, 2 + t % 2, :].rearrange("p (h n) -> p h n", h=HC)[:, :, 0:n],
                        SCALE, wt[0:n, :, 0:n], ALU.mult, ALU.mult).then_inc(at_ready.sem, 1)
                    k = kc[0:n, t, :].rearrange("p (h d) -> p h d", h=HC)
                    if t < 4:
                        if t:
                            ve.wait_ge(cu_done.sem, cu_done.at(L, t))
                        ve.tensor_tensor(kw[:], k, wt[:, :, P - 1:P].to_broadcast([P, HC, HD]), ALU.mult) \
                          .then_inc(kw_ready.sem, 1)
                    else:
                        for b in range(NB):
                            e = NT * b + NT - 1
                            ins = ve.tensor_tensor(kwm[:, b], k, wt[0:32, :, e:e + 1].to_broadcast([32, HC, HD]),
                                                   ALU.mult)
                        ins.then_inc(kw_ready.sem, 1)

                def finish(t):
                    n = P if t < 4 else 32
                    c = slice(t * P, t * P + n)
                    ve.wait_ge(nd_done.sem, nd_done.at(L, t + 1))
                    num, den = (psum[:, 4 + t % 2, 256 * i:256 * i + 256].rearrange("p (c n) -> p c n", c=2)[:, :, 0:n]
                                for i in range(2))
                    link(ve.scalar_tensor_tensor(dn[:, :, 0:n], den, -1.0, em[:, :, c], ALU.mult, ALU.max))
                    link(ve.tensor_tensor(dn[:, :, 0:n], den, dn[:, :, 0:n], ALU.max))
                    link(ve.reciprocal(dn[:, :, 0:n], dn[:, :, 0:n]))
                    ve.tensor_tensor(hc[:, :, c], num, dn[:, :, 0:n], ALU.mult).then_inc(hc_ready.sem, 1)

                def update(t):
                    ve.wait_ge(cu_done.sem, cu_done.at(L, t + 1))
                    if t >= 1:
                        ve.wait_ge(cu_ready.sem, cu_ready.at(L, t))
                    for p in range(2):
                        r = slice(HD * p, HD * p + HD)
                        new = psum[r, 6 + t % 2, 0:260].rearrange("p (c n) -> p c n", c=2)[:, :, 65 * p:65 * p + 65]
                        if t == 0:
                            ins = ve.tensor_copy(cp[r], new)
                        else:
                            for c in range(2):
                                ins = ve.scalar_tensor_tensor(cp[r, c, :], cp[r, c, :],
                                                              wi[r, c, t * P + P - 1:t * P + P], new[:, c, :],
                                                              ALU.mult, ALU.add)
                    ins.then_inc(cu_ready.sem, 1)

                for t in range(4):
                    weigh(t)
                    finish(t)
                    update(t)
                weigh(4)
                finish(4)
                ve.wait_ge(sc_loaded.sem, sc_loaded.at(L, 1))
                last = wi[:, :, SEQ:TOK].rearrange("p c (b t) -> p b c t", t=NT)[:, :, :, NT - 1:NT]
                for c in range(2):
                    ins = ve.tensor_tensor(cs[:, :, c, :], cs[:, :, c, :],
                                           last[:, :, c, :].to_broadcast([P, NB, HD + 1]), ALU.mult)
                link(ins)
                for b in range(NB):
                    ve.wait_ge(cu_done.sem, cu_done.at(L, 5 + b))
                    for p in range(2):
                        r = slice(HD * p, HD * p + HD)
                        new = psum[r, 6 + b % 2, 0:260].rearrange("p (c n) -> p c n", c=2)[:, :, 65 * p:65 * p + 65]
                        ins = ve.tensor_tensor(cs[r, b], cs[r, b], new, ALU.add)
                    ins.then_inc(cu_ready.sem, 1)
                ve.wait_ge(oc_ready.sem, oc_ready.at(L, 1))
                ve.wait_ge(hc_ready.sem, hc_ready.at(L, 5))
                ve.tensor_tensor(z[:, ZVC:ZVC + 2, :], hc[:], z[:, ZOC:ZOC + 2, :], ALU.mult).then_inc(c_done.sem, 1)

                def row_max(s, ready, out, scores, mask):
                    link(ve.tensor_tensor_reduce(out, scores, mask, 1.0, LOW, ALU.add, ALU.max, s[:, 0:1]))
                    ve.tensor_scalar(s[:, 1:2], s[:, 0:1], -SCALE, None, ALU.mult).then_inc(ready.sem, 1)

                def row_sum(s, ready, out, mask):
                    link(ve.tensor_tensor_reduce(out, out, mask, 1.0, 0.0, ALU.mult, ALU.add, s[:, 2:3]))
                    link(ve.reciprocal(s[:, 3:4], s[:, 2:3]))
                    ve.tensor_scalar(out, out, s[:, 3:4], None, ALU.mult).then_inc(ready.sem, 1)

                two = lambda v: v.rearrange("p (h n) -> p h n", h=2)
                ve.wait_ge(qz_ready.sem, qz_ready.at(L, 1))
                for c in range(3):
                    for p in range(2):
                        r = slice(HD * p, HD * p + HD)
                        o = 8 * c + 4 * p
                        ins = ve.tensor_copy(qbd[r, :, c, o:o + NT],
                                             z[r, ZQ + c, SEQ:TOK].rearrange("p (b t) -> p b t", t=NT))
                ins.then_inc(q_ready.sem, 1)
                ve.wait_ge(z_stored.sem, z_stored.at(L, 2))
                ve.nop(nofuse=True)
                for i in range(STEPS_A):
                    if i < 24:
                        n = (i % 4 + 1) * P
                        ve.wait_ge(s_done.sem, s_done.at(L, i + 1))
                        if i >= 2:
                            ve.wait_ge(pt_done.sem, pt_done.at(L, i - 1))
                        ve.nop(nofuse=True)
                        row_max(stat[:, i % 2], mx_ready, pp[:, i % 2, 0:n], psum[:, i % 2, 0:n],
                                con[:, K_PADD + SEQ - n:K_PADD + SEQ])
                    if 1 <= i < 25:
                        n = ((i - 1) % 4 + 1) * P
                        ve.wait_ge(e_ready.sem, e_ready.at(L, i))
                        row_sum(stat[:, (i - 1) % 2], p_done, pp[:, (i - 1) % 2, 0:n],
                                con[:, K_PMUL + SEQ - n:K_PMUL + SEQ])
                    if 3 <= i < 27:
                        u = i - 3
                        r = slice(HD * (u // 4 % 2), HD * (u // 4 % 2) + HD)
                        ve.wait_ge(o_done.sem, o_done.at(L, u + 1))
                        ve.tensor_copy(z[r, ZV + u // 8, u % 4 * P:(u % 4 + 1) * P], psum[r, 6 + u % 2, 0:P]) \
                          .then_inc(o_ready.sem, 1)
                    for g in range(2):
                        if i == S_MAX[g]:
                            ve.wait_ge(kv_used.sem, kv_used.at(L, 8 * g + 4))
                            if g:
                                ve.wait_ge(spt_done.sem, spt_done.at(L, 2))
                            ve.nop(nofuse=True)
                            row_max(stat[:, 2], smx_ready, two(ps_[:, :]), psum[:, 2:4, 0:KS // 2],
                                    two(con[:, K_SADD:K_SADD + KS]))
                        if i == S_SUM[g]:
                            ve.wait_ge(smx_ready.sem, smx_ready.at(L, g + 1))
                            ve.wait_ge(se_ready.sem, se_ready.at(L, g + 1))
                            row_sum(stat[:, 2], sp_done, ps_[:, :], con[:, K_SMUL:K_SMUL + KS])
                        if i == S_COPY[g]:
                            ve.wait_ge(kv_used.sem, kv_used.at(L, 8 * g + 8))
                            ve.tensor_copy(ps_[:, 0:384], psum[:, 2, 0:384]).then_inc(so_copied.sem, 1)
                        if i == S_OUT[g]:
                            ve.wait_ge(so_turned.sem, so_turned.at(L, g + 1))
                            for c in range(3):
                                for p in range(2):
                                    r = slice(HD * p, HD * p + HD)
                                    at = SEQ + KEYS_NEW * g
                                    o = psum[r, 3, c * P:(c + 1) * P].rearrange("p (j q) -> p j q", j=4)
                                    k = 8 * c + 4 * p
                                    ins = ve.tensor_copy(
                                        z[r, ZV + c, at:at + KEYS_NEW].rearrange("p (j t) -> p j t", t=NT),
                                        o[:, :, k:k + NT])
                            ins.then_inc(so_ready.sem, 1)

                def out_gain(k):
                    c = (G_A + k) if k < 3 else (G_B + k - 3) if k < 6 else (G_C + k - 6)
                    return pc[:, c:c + 1]
                ve.wait_ge(gr_ready.sem, gr_ready.at(L, 4))
                halves = lambda v: v.rearrange("p (h n) -> p h n", h=2)
                normed(L, N_OUT, lambda k: halves(z[:, OUT_TILES[k], :]), out_gain,
                       lambda k: gr[:, (0, 0, 0, 1, 1, 1, 2, 3)[k]])

            ve.memset(sp[:], 0.0).then_inc(layer_done.sem, 1)
            for free in (h_ready, hl_ready, y_ready, ye_ready):
                ve.sem_inc(free.sem, free.ahead)
            with ve.Fori(0, DEPTH) as L:
                steps = Steps(ve, dve_steps, L)
                ve.wait_ge(layer_done.sem, L + 1)
                prepare(L)
                pre_norm(L, N_F1, 0, G_F1PRE)
                gate_up(L, 0)
                out_tiles(L, 0, 0, y_ff)
                add_norm(L, 0, 1, y_ff, dc[:, D_HALF1:D_HALF1 + 8])
                pre_norm(L, N_MIX, 2, G_MIXPRE)
                mix_vector(L)
                out_tiles(L, KT, 1, y_z)
                add_norm(L, 1, 3, y_z, pc[:, G_MIXPOST:G_MIXPOST + 8])
                pre_norm(L, N_F2, 4, G_F2PRE)
                gate_up(L, 1)
                out_tiles(L, 2 * KT, 2, y_ff)
                ve.wait_ge(p_ready.sem, p_ready.at(L, 1))
                ve.tensor_tensor(pl[:], pe_raw[:], ph[:].bitcast(F32), ALU.subtract).then_inc(p_ready.sem, 1)
                add_norm(L, 2, 5, y_ff, dc[:, D_HALF2:D_HALF2 + 8])
                for d in range(4):
                    ve.wait_ge(pj_done.sem, pj_done.at(L, d + 1))
                    ve.tensor_copy(y_z[:, d], T(d % 4)).then_inc(pj_ready.sem, 1)
                pre_norm(L, N_PLE, 6, G_PLEPRE)
                for d in range(4, KT):
                    ve.wait_ge(pj_done.sem, pj_done.at(L, d + 1))
                    ve.tensor_copy(y_z[:, d], T(d % 4)).then_inc(pj_ready.sem, 1)
                ve.wait_ge(pj_ready.sem, pj_ready.at(L, KT))
                for d in range(KT):
                    ve.wait_ge(pg_ready.sem, pg_ready.at(L, d + 1))
                    ve.tensor_tensor(y_z[:, d], y_z[:, d], act_out[:, d % 2], ALU.mult).then_inc(ye_ready.sem, 1)
                    if d >= 2:
                        add_square(L, 3, d - 1)
                add_square(L, 3, KT - 1)
                add_norm(L, 3, 7, y_z, pc[:, G_PLEPOST:G_PLEPOST + 8])
                ve.wait_ge(xn_ready.sem, xn_ready.at(L, 32))
                ve.sem_inc(layer_done.sem, 1)
                steps.end()

        @block.gpsimd
        def _(po):
            def lo_part(k, hi_value):
                po.wait_ge(hi.sem, hi_value)
                po.tensor_tensor(wl[:, k, :], raw[:, k, :], wh[:, k, :].bitcast(F32), ALU.subtract) \
                  .then_inc(lo.sem, 1)

            def lo_parts(L, first, count):
                with po.Fori(0, count // 2) as f:
                    for k in range(2):
                        lo_part(k, hi.at(L, first + k + 3) + f * 2)

            po.sem_inc(z_ready.sem, z_ready.ahead)
            po.sem_inc(pg_ready.sem, pg_ready.ahead)
            lo_part(0, 1)
            lo_part(1, 2)
            with po.Fori(0, DEPTH) as L:
                steps = Steps(po, pool_steps, L)
                lo_parts(L, CH_F1, CH_OUT - CH_F1)
                for t in range(5):
                    n = P if t < 4 else 32
                    w = wt[0:n, :, 0:n]
                    po.wait_ge(we_ready.sem, we_ready.at(L, t + 1))
                    po.nop(nofuse=True)
                    causal = po.affine_select(out=w, in_=w, pattern=[[0, HC], [1, n]], compare_op=ALU.is_ge,
                                              fill=0.0, base=0, channel_multiplier=-1)
                    if t < 4:
                        causal.then_inc(wm_ready.sem, 1)
                    else:
                        steps.link(causal, hold=True)
                        w = w.rearrange("p h (b t) -> p h b t", t=NT)
                        po.affine_select(out=w, in_=w, pattern=[[0, HC], [-NT, NB], [0, NT]],
                                         compare_op=ALU.is_ge, fill=0.0, base=0, channel_multiplier=1) \
                          .then_inc(wm_ready.sem, 1)
                po.wait_ge(cu_done.sem, cu_done.at(L, 4 + NB))
                po.nop(nofuse=True)
                po.memset(qbd[:], 0.0).then_inc(qz_ready.sem, 1)
                lo_parts(L, CH_OUT, CHUNKS - CH_OUT)
                steps.end()


def reached():
    old = [16 * g + t for t in range(4) for g in range(96)]
    return np.array(old + list(range(W_BUF - 512, W_BUF)))


def constants():
    c = np.zeros((P, NCONST), np.float32)
    c[:, K_ID:K_ID + P] = np.eye(P)
    c[:, K_ONE:K_ONE + P] = 1.0
    c[:64, K_BLK:K_BLK + 64] = 1.0
    c[64:, K_BLK + 64:K_BLK + 128] = 1.0

    def count(dist):
        return (((dist >= 0) & (dist <= 128)).astype(int)
                + ((dist >= 0) & (dist <= 512) & (dist % 4 == 0))
                + ((dist >= 0) & (dist <= 2048) & (dist % 16 == 0)))

    n = count(np.arange(P)[:, None] - (np.arange(SEQ)[None] - (SEQ - P)))
    c[:, K_PADD:K_PADD + SEQ] = np.where(n > 0, 0.0, NEG)
    c[:, K_PMUL:K_PMUL + SEQ] = n
    rows = reached()
    for j in range(4):
        for r in range(24):
            t = r % 4
            n = np.concatenate([count(W_BUF + t - rows), np.zeros(KEYS_NEW, int)])
            n[KEYS + 4 * j:KEYS + 4 * j + 4] = count(t - np.arange(4))
            c[32 * j + r, K_SADD:K_SADD + KS] = np.where(n > 0, 0.0, NEG)
            c[32 * j + r, K_SMUL:K_SMUL + KS] = n
        c[32 * j + 24:32 * j + 32, K_SMUL:K_SMUL + KS] = 1.0
    for h in range(HC):
        c[h, K_SELH + h * P:K_SELH + (h + 1) * P] = 1.0
        o = K_SEL2 + (h // 2) * P + (h % 2) * HD
        c[h, o:o + HD] = 1.0
    keep = np.ones(TOK, np.float32)
    keep[0:SEQ:P] = 0.0
    keep[SEQ::NT] = 0.0
    c[:, K_RST:K_RST + TOK] = keep
    return c


def lay_out(i):
    f32 = np.float32
    out = {}

    def feature_major(prompt, sample):
        a = np.concatenate([prompt.reshape(SEQ, -1), sample.reshape(NB * NT, -1)]).T
        return a.reshape(-1, P, 2, HALF).transpose(1, 0, 2, 3)

    out["x"] = feature_major(i["x_prompt"][0], i["x_sample"])
    out["pe"] = np.stack([feature_major(i["p_prompt"][l, 0], i["p_sample"][l]) for l in range(DEPTH)])

    w = np.zeros((DEPTH * CHUNKS + 2, P, 8, P), f32)
    splits = np.cumsum([0, 384, 384, 384, 384, 384, 256, 256, 256, 256, 4, 4])
    for l in range(DEPTH):
        o = l * CHUNKS
        for c0, g, u, d, c1 in ((CH_F1, "w_f1_gate", "w_f1_up", "w_f1_down", CH_D1),
                                (CH_F2, "w_f2_gate", "w_f2_up", "w_f2_down", CH_D2)):
            for n, name in enumerate((g, u)):
                w[o + c0 + n:o + c0 + C_UP:2] = i[name][l].reshape(KT, P, FT, P).transpose(2, 1, 0, 3)
            b = i[d][l].reshape(FT, P, KT, P).transpose(2, 1, 0, 3)
            at = 0
            for p, n in enumerate(DOWN_BLOCKS):
                w[o + c1 + p:o + c1 + C_DOWN:3, :, 0:n] = b[:, :, at:at + n]
                at += n
        s = i["w_in"][l]
        part = [s[:, splits[n]:splits[n + 1]] for n in range(11)]
        q, k, v, xb, gb, qc, kc, vc, oc, ic, fc = part
        gates = np.zeros((D, P), f32)
        gates[:, 0:4], gates[:, 32:36] = ic, fc
        s = np.concatenate([xb, gb, gates, qc, kc, vc, oc, q, k, v], axis=1)
        w[o + CH_IN:o + CH_IN + NZ] = s.reshape(KT, P, NZ, P).transpose(2, 1, 0, 3)
        for c0, name in ((CH_OUT, "w_out"), (CH_PG, "w_ple_gate")):
            w[o + c0:o + c0 + KT] = i[name][l].reshape(KT, P, KT, P).transpose(2, 1, 0, 3)
        b = i["w_ple_proj"][l].reshape(2, P, 2, 4, P).transpose(2, 1, 3, 0, 4)
        w[o + CH_PJ:o + CH_PJ + 2] = b.reshape(2, P, 8, P)
    out["weights"] = w.reshape(-1, P, 8 * P)

    par = np.zeros((DEPTH, P, NPAR), f32)

    def column(c, name):
        a = i[name].reshape(DEPTH, -1, P)
        par[:, :, c:c + a.shape[1]] = a.transpose(0, 2, 1)

    for c, name in ((G_F1PRE, "g_f1_pre"), (G_F1POST, "g_f1_post"), (G_MIXPRE, "g_mix_pre"),
                    (G_MIXPOST, "g_mix_post"), (G_F2PRE, "g_f2_pre"), (G_F2POST, "g_f2_post"),
                    (G_PLEPRE, "g_ple_pre"), (G_PLEPOST, "g_ple_post"), (CONV_W, "conv_w"), (CONV_B, "conv_b"),
                    (B_RA, "b_rg_a"), (B_RX, "b_rg_x"), (LAM, "lru_lambda"), (G_A, "g_out_a"),
                    (G_B, "g_out_b"), (G_C, "g_out_c")):
        column(c, name)
    par[:, 0:HC, B_I] = i["b_mlstm_i"]
    par[:, 32:32 + HC, B_F] = i["b_mlstm_f"]
    out["par"] = par
    rgw = np.zeros((DEPTH, P, 2, 3, P), f32)
    for n, name in enumerate(("w_rg_a", "w_rg_x")):
        for j in range(3):
            for p in range(2):
                rgw[:, 64 * p:64 * p + 64, n, j, 64 * p:64 * p + 64] = i[name][:, 2 * j + p]
    out["rgw"] = rgw
    out["consts"] = constants()

    rows = reached()
    k = i["cache_k"][:, :, rows].reshape(DEPTH, NB, KEYS, 3, P)
    out["kc"] = k.transpose(0, 1, 4, 3, 2).reshape(DEPTH, NB, P, 3 * KEYS)
    v = i["cache_v"][:, :, rows].reshape(DEPTH, NB, 7, P, 384)
    out["vc"] = v.transpose(0, 1, 3, 2, 4).reshape(DEPTH, NB, P, 7 * 384)
    out["sconv"] = i["state_conv"].reshape(DEPTH, NB, 3, 3, P).transpose(0, 4, 3, 1, 2)
    out["sh"] = i["state_h"].reshape(DEPTH, NB, 3, P).transpose(0, 3, 2, 1)
    c = np.concatenate([i["state_C"], i["state_n"][..., None]], axis=-1)
    out["sc"] = c.reshape(DEPTH, NB, 2, 2, HD, HD + 1).transpose(0, 3, 4, 1, 2, 5).reshape(DEPTH, P, NB, 2, HD + 1)
    out["sm"] = i["state_m"].transpose(0, 2, 1)
    return {n: np.ascontiguousarray(a) for n, a in out.items()}


OUTPUTS = dict(x=(P, KT, 2, HALF), k=(DEPTH, P, 3, TOK), v=(DEPTH, P, 3, TOK), sb=(DEPTH, P, NSB),
               cp=(DEPTH, P, 2, HD + 1), cs=(DEPTH, P, NB, 2, HD + 1), m=(DEPTH, HC, 1 + NB))


def kernel(**inputs):
    import concourse.bacc as bacc
    from concourse.bass_utils import run_bass_kernel_spmd

    arrays = lay_out({n: np.asarray(a) for n, a in inputs.items()})
    nc = bacc.Bacc("TRN2", target_bir_lowering=False, num_devices=1)
    ins = {n: nc.dram_tensor(f"in_{n}", list(a.shape), F32, kind="ExternalInput").ap() for n, a in arrays.items()}
    outs = {n: nc.dram_tensor(f"out_{n}", list(s), F32, kind="ExternalOutput").ap() for n, s in OUTPUTS.items()}
    build(nc, ins, outs)
    r = run_bass_kernel_spmd(nc, [{f"in_{n}": a for n, a in arrays.items()}], core_ids=[0])
    o = {n: np.asarray(r.results[0][f"out_{n}"]) for n in OUTPUTS}

    y = o["x"].transpose(1, 0, 2, 3).reshape(D, TOK).T
    y_prompt, y_sample = y[None, :SEQ], y[SEQ:].reshape(NB, NT, D)

    def rows_of(a):
        t = a.transpose(0, 3, 2, 1).reshape(DEPTH, TOK, HA, HD)
        return t[:, None, :SEQ], t[:, SEQ:].reshape(DEPTH, NB, NT, HA, HD)

    k_prompt, k_sample = rows_of(o["k"])
    v_prompt, v_sample = rows_of(o["v"])
    s = o["sb"]
    conv_prompt = s[:, :, S_CP:S_CS].reshape(DEPTH, P, 3, 3).transpose(0, 3, 2, 1).reshape(DEPTH, 1, 3, DB)
    conv_sample = s[:, :, S_CS:S_HP].reshape(DEPTH, P, 3, NB, 3).transpose(0, 3, 4, 2, 1).reshape(DEPTH, NB, 3, DB)
    h_prompt = s[:, :, S_HP:S_HS].transpose(0, 2, 1).reshape(DEPTH, 1, DB)
    h_sample = s[:, :, S_HS:NSB].reshape(DEPTH, P, 3, NB).transpose(0, 3, 2, 1).reshape(DEPTH, NB, DB)
    cp = o["cp"].reshape(DEPTH, 2, HD, 2, HD + 1).transpose(0, 3, 1, 2, 4).reshape(DEPTH, 1, HC, HD, HD + 1)
    cs = o["cs"].reshape(DEPTH, 2, HD, NB, 2, HD + 1).transpose(0, 3, 4, 1, 2, 5).reshape(DEPTH, NB, HC, HD, HD + 1)
    m_prompt = o["m"][:, :, 0][:, None]
    m_sample = o["m"][:, :, 1:].transpose(0, 2, 1)
    out = (y_prompt, y_sample, k_prompt, v_prompt, k_sample, v_sample, conv_prompt, conv_sample,
           h_prompt, h_sample, cp[..., :HD], cs[..., :HD], cp[..., HD], cs[..., HD], m_prompt, m_sample)
    return tuple(np.ascontiguousarray(a) for a in out)
```
